# Optimizing a Trainium2 kernel written in Bass

```python
import math
import jax, jax.numpy as jnp
from jax import lax
import numpy as np

D_MODEL = 1024
BATCH = 1
SEQ = 256
DEPTH = 1
DEC_BATCH = 8
DEC_SEQ = 8
PAST_LEN = 1024
PAGE_SIZE = 128

HEAD_DIM = 64
MIX_WIDTH = D_MODEL
SB_WIDTH = MIX_WIDTH // 2
DIFF_WIDTH = MIX_WIDTH - SB_WIDTH
SB_HEADS = SB_WIDTH // HEAD_DIM
DIFF_HEADS = DIFF_WIDTH // (2 * HEAD_DIM)
PROJ_WIDTH = 3 * SB_WIDTH + 3 * DIFF_WIDTH
N_EXPERTS = 32
TOP_K = 4
D_FF = D_MODEL
SWIGLU_LIMIT = 7.0
SWIGLU_ALPHA = 1.702
Q_BLOCK = 128
EXPERT_BLOCK = 128
LN_EPS = 1e-5
DEEPNORM_ALPHA = (2.0 * DEPTH) ** 0.25
DEEPNORM_BETA = (8.0 * DEPTH) ** -0.25
NEG_INF = -1e30

kernel_name = "hybrid_sb_diff_moe_deepnorm_step"

def layer_norm(x, g, b):
    xf = x.astype(jnp.float32)
    mu = jnp.mean(xf, axis=-1, keepdims=True)
    var = jnp.mean(jnp.square(xf - mu), axis=-1, keepdims=True)
    return ((xf - mu) * lax.rsqrt(var + LN_EPS) * g.astype(jnp.float32) + b.astype(jnp.float32)).astype(x.dtype)

def rms_norm(x, g):
    xf = x.astype(jnp.float32)
    ms = jnp.mean(jnp.square(xf), axis=-1, keepdims=True)
    return (xf * lax.rsqrt(ms + LN_EPS) * g.astype(jnp.float32)).astype(x.dtype)

def alibi_slopes(n_heads):
    h = jnp.arange(1, n_heads + 1, dtype=jnp.float32)
    return jnp.exp2(-8.0 * h / n_heads)

def query_blocks(q, q_pos):
    B, T = q.shape[0], q.shape[1]
    qb = min(Q_BLOCK, T)
    nb = -(-T // qb)
    pad = nb * qb - T
    q = jnp.pad(q, [(0, 0), (0, pad)] + [(0, 0)] * (q.ndim - 2))
    q_pos = jnp.pad(q_pos, (0, pad), mode="edge")
    q = jnp.moveaxis(q.reshape((B, nb, qb) + q.shape[2:]), 1, 0)
    return q, q_pos.reshape(nb, qb), T

def merge_blocks(o, T):
    o = jnp.moveaxis(o, 0, 1)
    o = o.reshape((o.shape[0], o.shape[1] * o.shape[2]) + o.shape[3:])
    return o[:, :T]

def stick_breaking_attention(q, k, v, q_pos, k_pos):
    scale = HEAD_DIM ** -0.5
    qblk, pblk, T = query_blocks(q, q_pos)

    def one_block(args):
        qb, pb = args
        z = jnp.einsum("bqhd,bkhd->bhqk", qb, k, preferred_element_type=jnp.float32) * scale
        mask = k_pos[None, :] < pb[:, None]
        log_1m = jnp.where(mask, jax.nn.log_sigmoid(-z), 0.0)
        log_rest = lax.cumsum(log_1m, axis=3, reverse=True) - log_1m
        w = jnp.where(mask, jnp.exp(jax.nn.log_sigmoid(z) + log_rest), 0.0)
        return jnp.einsum("bhqk,bkhd->bqhd", w.astype(v.dtype), v)

    return merge_blocks(lax.map(one_block, (qblk, pblk)), T)

def differential_attention(q, k, v, q_pos, k_pos, lam, slopes):
    scale = HEAD_DIM ** -0.5
    qblk, pblk, T = query_blocks(q, q_pos)

    def one_block(args):
        qb, pb = args
        z = jnp.einsum("bqhcd,bkhcd->bchqk", qb, k, preferred_element_type=jnp.float32) * scale
        dist = (pb[:, None] - k_pos[None, :]).astype(jnp.float32)
        z = z - slopes[:, None, None] * dist[None]
        z = jnp.where(dist >= 0.0, z, NEG_INF)
        p = jax.nn.softmax(z, axis=-1)
        a = p[:, 0] - lam * p[:, 1]
        return jnp.einsum("bhqk,bkhe->bqhe", a.astype(v.dtype), v)

    return merge_blocks(lax.map(one_block, (qblk, pblk)), T)

def token_mixer(h, past, w_in, lam_q1, lam_k1, lam_q2, lam_k2, subln_g, w_out, lambda_init):
    B, T, _ = h.shape
    proj = jnp.einsum("btd,de->bte", h, w_in)
    splits = [SB_WIDTH, 2 * SB_WIDTH, 3 * SB_WIDTH, 3 * SB_WIDTH + DIFF_WIDTH, 3 * SB_WIDTH + 2 * DIFF_WIDTH]
    sb_q, sb_k, sb_v, d_q, d_k, d_v = jnp.split(proj, splits, axis=-1)
    sb_q = sb_q.reshape(B, T, SB_HEADS, HEAD_DIM)
    sb_k = sb_k.reshape(B, T, SB_HEADS, HEAD_DIM)
    sb_v = sb_v.reshape(B, T, SB_HEADS, HEAD_DIM)
    d_q = d_q.reshape(B, T, DIFF_HEADS, 2, HEAD_DIM)
    d_k = d_k.reshape(B, T, DIFF_HEADS, 2, HEAD_DIM)
    d_v = d_v.reshape(B, T, DIFF_HEADS, 2 * HEAD_DIM)
    new_rows = (sb_k, sb_v, d_k, d_v)
    if past is None:
        P = 0
        keys = new_rows
    else:
        P = past[0].shape[1]
        keys = (jnp.concatenate([past[0], sb_k], axis=1), jnp.concatenate([past[1], sb_v], axis=1),
                jnp.concatenate([past[2], d_k], axis=1), jnp.concatenate([past[3], d_v], axis=1))
    q_pos = P + jnp.arange(T, dtype=jnp.int32)
    k_pos = jnp.arange(P + T, dtype=jnp.int32)

    sb_out = stick_breaking_attention(sb_q, keys[0], keys[1], q_pos, k_pos)
    lam = (jnp.exp(jnp.sum(lam_q1.astype(jnp.float32) * lam_k1.astype(jnp.float32)))
           - jnp.exp(jnp.sum(lam_q2.astype(jnp.float32) * lam_k2.astype(jnp.float32))) + lambda_init)
    d_out = differential_attention(d_q, keys[2], keys[3], q_pos, k_pos, lam, alibi_slopes(DIFF_HEADS))
    d_out = rms_norm(d_out, subln_g) * (1.0 - lambda_init)
    mixed = jnp.concatenate([sb_out.reshape(B, T, SB_WIDTH), d_out.reshape(B, T, DIFF_WIDTH)], axis=-1)
    return jnp.einsum("btm,md->btd", mixed, w_out), new_rows

def moe_ffn(x2d, w_router, b_router, w_gate_up, b_gate_up, w_down, b_down):
    n = x2d.shape[0]
    logits = jnp.einsum("nd,de->ne", x2d, w_router, preferred_element_type=jnp.float32) + b_router.astype(jnp.float32)
    top_vals, top_idx = lax.top_k(logits, TOP_K)
    gates = jax.nn.softmax(top_vals, axis=-1)
    flat_e = top_idx.reshape(-1)
    flat_tok = jnp.repeat(jnp.arange(n, dtype=jnp.int32), TOP_K)
    flat_g = gates.reshape(-1)
    order = jnp.argsort(flat_e)
    se, stok, sg = flat_e[order], flat_tok[order], flat_g[order]
    counts = jnp.bincount(flat_e, length=N_EXPERTS)
    padded = ((counts + EXPERT_BLOCK - 1) // EXPERT_BLOCK) * EXPERT_BLOCK
    pend = jnp.cumsum(padded)
    pstart = pend - padded
    ustart = jnp.cumsum(counts) - counts
    dest = pstart[se] + (jnp.arange(n * TOP_K, dtype=jnp.int32) - ustart[se])
    n_rows = -(-(n * TOP_K + N_EXPERTS * (EXPERT_BLOCK - 1)) // EXPERT_BLOCK) * EXPERT_BLOCK
    n_blocks = n_rows // EXPERT_BLOCK
    row_tok = jnp.zeros((n_rows,), jnp.int32).at[dest].set(stok)
    row_gate = jnp.zeros((n_rows,), jnp.float32).at[dest].set(sg)
    block_start = jnp.arange(n_blocks, dtype=jnp.int32) * EXPERT_BLOCK
    block_expert = jnp.clip(jnp.searchsorted(pend, block_start, side="right"), 0, N_EXPERTS - 1)

    def expert_block(args):
        toks, e = args
        xb = x2d[toks]
        gu = xb @ w_gate_up[e] + b_gate_up[e]
        g, u = gu[:, :D_FF], gu[:, D_FF:]
        g = jnp.minimum(g, SWIGLU_LIMIT)
        u = jnp.clip(u, -SWIGLU_LIMIT, SWIGLU_LIMIT)
        hid = (u + 1.0) * (g * jax.nn.sigmoid(SWIGLU_ALPHA * g))
        return hid @ w_down[e] + b_down[e]

    out = lax.map(expert_block, (row_tok.reshape(n_blocks, EXPERT_BLOCK), block_expert))
    out = out.reshape(n_rows, -1).astype(jnp.float32) * row_gate[:, None]
    y = jnp.zeros((n, x2d.shape[1]), jnp.float32).at[row_tok].add(out)
    return y.astype(x2d.dtype)

def decoder_layer(x, past, w_in, lam_q1, lam_k1, lam_q2, lam_k2, subln_g, w_out, ln1_g, ln1_b,
                  w_router, b_router, w_gate_up, b_gate_up, w_down, b_down, ln2_g, ln2_b, lambda_init):
    mix_out, new_rows = token_mixer(x, past, w_in, lam_q1, lam_k1, lam_q2, lam_k2, subln_g, w_out, lambda_init)
    x = layer_norm(DEEPNORM_ALPHA * x + mix_out, ln1_g, ln1_b)
    B, T, D = x.shape
    ffn = moe_ffn(x.reshape(B * T, D), w_router, b_router, w_gate_up, b_gate_up, w_down, b_down).reshape(B, T, D)
    x = layer_norm(DEEPNORM_ALPHA * x + ffn, ln2_g, ln2_b)
    return x, new_rows

def gather_pages(pool, layer, page_table):
    g = pool[layer, page_table]
    return g.reshape((g.shape[0], g.shape[1] * g.shape[2]) + g.shape[3:])

def setup_inputs(seed: int = 0) -> dict:
    key = jax.random.key(seed)
    ks = jax.random.split(key, 24)
    n_pages = PAST_LEN // PAGE_SIZE
    n_used = DEC_BATCH * n_pages
    n_pool = n_used + -(-n_used // 4)
    nrm = jax.random.normal
    x_prompt = nrm(ks[0], (BATCH, SEQ, D_MODEL), jnp.float32)
    x_sample = nrm(ks[1], (DEC_BATCH, DEC_SEQ, D_MODEL), jnp.float32)
    cache_sb_k = nrm(ks[2], (DEPTH, n_pool, PAGE_SIZE, SB_HEADS, HEAD_DIM), jnp.float32)
    cache_sb_v = nrm(ks[3], (DEPTH, n_pool, PAGE_SIZE, SB_HEADS, HEAD_DIM), jnp.float32) * DEEPNORM_BETA
    cache_diff_k = nrm(ks[4], (DEPTH, n_pool, PAGE_SIZE, DIFF_HEADS, 2, HEAD_DIM), jnp.float32)
    cache_diff_v = nrm(ks[5], (DEPTH, n_pool, PAGE_SIZE, DIFF_HEADS, 2 * HEAD_DIM), jnp.float32) * DEEPNORM_BETA
    page_table = jax.random.permutation(ks[6], n_pool)[:n_used].reshape(DEC_BATCH, n_pages).astype(jnp.int32)
    col_scale = jnp.concatenate([jnp.ones((2 * SB_WIDTH,), jnp.float32), jnp.full((SB_WIDTH,), DEEPNORM_BETA, jnp.float32),
                                 jnp.ones((2 * DIFF_WIDTH,), jnp.float32), jnp.full((DIFF_WIDTH,), DEEPNORM_BETA, jnp.float32)])
    w_in = nrm(ks[7], (DEPTH, D_MODEL, PROJ_WIDTH), jnp.float32) * D_MODEL ** -0.5 * col_scale
    lambda_q1 = 0.1 * nrm(ks[8], (DEPTH, HEAD_DIM), jnp.float32)
    lambda_k1 = 0.1 * nrm(ks[9], (DEPTH, HEAD_DIM), jnp.float32)
    lambda_q2 = 0.1 * nrm(ks[10], (DEPTH, HEAD_DIM), jnp.float32)
    lambda_k2 = 0.1 * nrm(ks[11], (DEPTH, HEAD_DIM), jnp.float32)
    subln_g = 1.0 + 0.1 * nrm(ks[12], (DEPTH, 2 * HEAD_DIM), jnp.float32)
    w_out = nrm(ks[13], (DEPTH, MIX_WIDTH, D_MODEL), jnp.float32) * MIX_WIDTH ** -0.5 * DEEPNORM_BETA
    ln1_g = 1.0 + 0.1 * nrm(ks[14], (DEPTH, D_MODEL), jnp.float32)
    ln1_b = 0.02 * nrm(ks[15], (DEPTH, D_MODEL), jnp.float32)
    w_router = nrm(ks[16], (DEPTH, D_MODEL, N_EXPERTS), jnp.float32) * D_MODEL ** -0.5
    b_router = 0.01 * nrm(ks[17], (DEPTH, N_EXPERTS), jnp.float32)
    w_gate_up = nrm(ks[18], (DEPTH, N_EXPERTS, D_MODEL, 2 * D_FF), jnp.float32) * D_MODEL ** -0.5 * DEEPNORM_BETA
    b_gate_up = 0.01 * nrm(ks[19], (DEPTH, N_EXPERTS, 2 * D_FF), jnp.float32)
    w_down = nrm(ks[20], (DEPTH, N_EXPERTS, D_FF, D_MODEL), jnp.float32) * D_FF ** -0.5 * DEEPNORM_BETA
    b_down = 0.01 * nrm(ks[21], (DEPTH, N_EXPERTS, D_MODEL), jnp.float32)
    ln2_g = 1.0 + 0.1 * nrm(ks[22], (DEPTH, D_MODEL), jnp.float32)
    ln2_b = 0.02 * nrm(ks[23], (DEPTH, D_MODEL), jnp.float32)
    return {"x_prompt": x_prompt, "x_sample": x_sample,
            "cache_sb_k": cache_sb_k, "cache_sb_v": cache_sb_v,
            "cache_diff_k": cache_diff_k, "cache_diff_v": cache_diff_v,
            "page_table": page_table, "w_in": w_in,
            "lambda_q1": lambda_q1, "lambda_k1": lambda_k1, "lambda_q2": lambda_q2, "lambda_k2": lambda_k2,
            "subln_g": subln_g, "w_out": w_out, "ln1_g": ln1_g, "ln1_b": ln1_b,
            "w_router": w_router, "b_router": b_router, "w_gate_up": w_gate_up, "b_gate_up": b_gate_up,
            "w_down": w_down, "b_down": b_down, "ln2_g": ln2_g, "ln2_b": ln2_b}

def reference(x_prompt, x_sample, cache_sb_k, cache_sb_v, cache_diff_k, cache_diff_v, page_table, w_in,
              lambda_q1, lambda_k1, lambda_q2, lambda_k2, subln_g, w_out, ln1_g, ln1_b,
              w_router, b_router, w_gate_up, b_gate_up, w_down, b_down, ln2_g, ln2_b):
    yp, ys = x_prompt, x_sample
    p_sbk, p_sbv, p_dk, p_dv = [], [], [], []
    s_sbk, s_sbv, s_dk, s_dv = [], [], [], []
    for i in range(DEPTH):
        lambda_init = 0.8 - 0.6 * math.exp(-0.3 * i)
        lw = (w_in[i], lambda_q1[i], lambda_k1[i], lambda_q2[i], lambda_k2[i], subln_g[i], w_out[i], ln1_g[i], ln1_b[i],
              w_router[i], b_router[i], w_gate_up[i], b_gate_up[i], w_down[i], b_down[i], ln2_g[i], ln2_b[i])
        past = (gather_pages(cache_sb_k, i, page_table), gather_pages(cache_sb_v, i, page_table),
                gather_pages(cache_diff_k, i, page_table), gather_pages(cache_diff_v, i, page_table))
        yp, rows_p = decoder_layer(yp, None, *lw, lambda_init)
        ys, rows_s = decoder_layer(ys, past, *lw, lambda_init)
        p_sbk.append(rows_p[0]); p_sbv.append(rows_p[1]); p_dk.append(rows_p[2]); p_dv.append(rows_p[3])
        s_sbk.append(rows_s[0]); s_sbv.append(rows_s[1]); s_dk.append(rows_s[2]); s_dv.append(rows_s[3])
    return (yp, ys,
            jnp.stack(p_sbk), jnp.stack(p_sbv), jnp.stack(p_dk), jnp.stack(p_dv),
            jnp.stack(s_sbk), jnp.stack(s_sbv), jnp.stack(s_dk), jnp.stack(s_dv))


_drawn_inputs = setup_inputs


def setup_inputs(seed=0):
    import zlib

    import numpy as np

    out = dict(_drawn_inputs(seed))
    spreads = {}
    factors = {'lambda_k1': 31.029,
     'lambda_q2': 26.94,
     'b_router': 19.487,
     'b_gate_up': 26.338,
     'b_down': 8.0,
     'ln2_b': 2.922}
    for name, (base, spread) in spreads.items():
        noise = np.random.default_rng([zlib.crc32(name.encode()), seed]).standard_normal(out[name].shape)
        drawn = base * np.exp(spread * noise) if base else spread * noise
        out[name] = __import__('jax').numpy.asarray(drawn.astype(out[name].dtype))
    for name, factor in factors.items():
        out[name] = (out[name] * factor).astype(out[name].dtype)
    return out
```

```python
from contextlib import ExitStack

import numpy as np
import concourse.bass as bass
from concourse import mybir

ALU = mybir.AluOpType
ACT = mybir.ActivationFunctionType
AX = mybir.AxisListType
F32 = mybir.dt.float32
I32 = mybir.dt.int32
U32 = mybir.dt.uint32

P = 128
D = 1024
KD = D // P
PROMPT, DEC_B, DEC_T = 256, 8, 8
SAMPLES = DEC_B * DEC_T
TOKENS = PROMPT + SAMPLES
BLOCKS = [(0, 128), (128, 128), (256, 64)]
PROJ = 3 * D
HD = 64
PAST, PAGE = 1024, 128
PAGES = PAST // PAGE
EXPERTS, TOP_K = 32, 4
SLOTS = 64
MAX_EXTRA = (TOKENS * TOP_K) // SLOTS - 1
TABLE_ITEMS = 64
BANK = 512
SLOT = 2048
RING = 12
SEED = 1
LIMIT, SIG_ALPHA = 7.0, 1.702
EPS = 1e-5
DEEP = 2.0 ** 0.25
LAM_INIT = 0.8 - 0.6
Q_SCALE = HD ** -0.5
NEG = -1e30
SLOPES = [2.0 ** (-8.0 * (h + 1) / 4) for h in range(4)]

CONST = {}
_at = 0
for _name, _n in (("ident", P), ("before", P), ("pdist", 256), ("pmask", 256), ("pneg", 256), ("sbias", PAST),
                  ("nbias", 120), ("nmask", 120), ("nneg", 120), ("expert", EXPERTS), ("token2", 3),
                  ("half", 1), ("is_c0", 1), ("is_c1", 1), ("row", 1)):
    CONST[_name] = (_at, _n)
    _at += _n
CONST_W = _at


def constants():
    t = np.zeros((P, CONST_W), np.float32)

    def put(name, a):
        at, n = CONST[name]
        t[:, at:at + n] = a
    i, j = np.arange(P)[:, None], np.arange(P)[None, :]
    put("ident", i == j)
    put("before", i < j)
    k = np.arange(256)[None, :]
    put("pdist", np.where(k <= 128 + i, k - (128.0 + i), -1e35))
    put("pmask", k < 128 + i)
    put("pneg", np.where(k < 128 + i, 0.0, NEG))
    group, c, q = i // 32, (i % 32) // 8, i % 8
    real = c < 2
    slope = np.array(SLOPES)[group]
    put("sbias", np.where(real, slope * (np.arange(PAST)[None, :] - (PAST + q)), 0.0))
    n = np.arange(120)[None, :] - 56
    own = (n >= 0) & (n < 8)
    put("nbias", np.where(own & (n <= q), slope * (n - q), NEG))
    put("nmask", own & (n < q))
    put("nneg", np.where(own & (n < q), 0.0, NEG))
    put("expert", np.arange(EXPERTS)[None, :])
    put("token2", 2 * (i + np.array([[b[0] for b in BLOCKS]])))
    put("half", i // 64)
    put("is_c0", c == 0)
    put("is_c1", c == 1)
    put("row", i)
    return t


class Count:

    def __init__(self, eng, sem, per=None):
        self.eng, self.sem, self.per, self.n, self.turn = eng, sem, per, 0, None

    def enter(self, turn, per=None):
        self.turn, self.per, self.first = turn, per if per is not None else self.per, self.n

    def leave(self, turns):
        assert self.n - self.first == self.per, (self.sem, self.n - self.first, self.per)
        self.n = self.first + self.per * turns
        self.turn = None

    def wait(self, back=0):
        v = self.n - back
        self.eng.wait_ge(self.sem, v if self.turn is None else self.turn * self.per + v)

    def next(self, k=1):
        self.n += k
        self.wait()

    def mark(self, ins, k=1):
        ins.then_inc(self.sem, k)
        self.n += k
        return self

    def link(self, ins):
        self.mark(ins)
        self.wait()


def decoder_step(nc, a, out, consts, scratch):
    x_dram = {0: a["x_prompt"][0, 0:128, :], 1: a["x_prompt"][0, 128:256, :],
              2: a["x_sample"].rearrange("b t d -> (b t) d")}
    w_in = a["w_in"][0]
    x1_dram, slot_dram, y_dram, extra_dram = scratch

    with ExitStack() as ctx:
        arena = ctx.enter_context(nc.sbuf_tensor("arena", [P, 52800], F32))
        small_i = ctx.enter_context(nc.sbuf_tensor("small_i", [P, 224], I32))
        psum = ctx.enter_context(nc.psum_tensor("psum", [P, 8, BANK], F32))
        top = [0]

        def sem(name):
            return ctx.enter_context(nc.semaphore(name))

        def room(n, at=None):
            start = top[0] if at is None else at
            if at is None:
                top[0] += n
            assert start + n <= 52800, start + n
            return arena[:, start:start + n]

        ring = room(RING * SLOT)
        slot = [ring[:, s * SLOT:(s + 1) * SLOT] for s in range(RING)]
        tab = room(CONST_W)
        mixT = room(8 * TOKENS).rearrange("p (k t) -> p k t", k=8)
        lam_cols = room(8)
        after_mix = top[0]
        const = {n: tab[:, at:at + w] for n, (at, w) in CONST.items()}
        ident = const["ident"]

        x_in = room(3 * D).rearrange("p (b d) -> p b d", b=3)
        xT = room(KD * TOKENS).rearrange("p (k t) -> p k t", k=KD)
        proj_end = top[0]
        top[0] = after_mix
        v_new = room(3 * D).rearrange("p (b d) -> p b d", b=3)
        qkT = room(4 * 4 * TOKENS).rearrange("p (n h t) -> p n h t", n=4, h=4)
        q_all = room(DEC_B * 2 * P).rearrange("p (b y r) -> p b y r", b=DEC_B, y=2)
        att_at = top[0]
        top[0] = att_at
        x_in = room(3 * D).rearrange("p (b d) -> p b d", b=3)
        xT = room(KD * TOKENS).rearrange("p (k t) -> p k t", k=KD)
        qk_rows = room(3 * 2 * D).rearrange("p (b d) -> p b d", b=3)
        proj_end = top[0]

        w_sem = [sem(f"w_in_loaded{k}") for k in range(KD)]
        x_loaded = [sem(f"x_loaded{b}") for b in range(3)]
        tab_loaded = sem("tab_loaded")
        ident_loaded = sem("ident_loaded")
        lam_loaded = sem("lam_loaded")
        pe_done = sem("pe_done")
        act_done = sem("act_done")
        dve_done = sem("dve_done")
        pool_done = sem("pool_done")
        w_in_used = sem("w_in_used")
        rows_out = sem("rows_out")
        page_loaded = [sem(f"page_loaded{s}") for s in range(8)]
        slot_used = [sem(f"slot_used{s}") for s in range(RING)]

        w_loaded = [sem(f"w_loaded{s}") for s in range(RING)]
        w_out_loaded = sem("w_out_loaded")
        turned = sem("turned")
        act_own, dve_own = sem("act_own"), sem("dve_own")
        caches = [a[n][0].rearrange(r) for n, r in (
            ("cache_sb_k", "n s h d -> n s (h d)"), ("cache_diff_k", "n s h c d -> n s (h c d)"),
            ("cache_sb_v", "n s h d -> n s (h d)"), ("cache_diff_v", "n s h d -> n s (h d)"))]
        TURNS = 22

        def past_used(sp, b, s):
            if s < 4:
                sp.wait_ge(turned, TURNS * b + (4 * (s + 1) - TURNS))
            else:
                sp.wait_ge(slot_used[s], b)

        def load_pages(sp, b, s, reuse=False):
            pages = [sp.value_load(a["page_table"][bass.ds(b, 1), 4 * (s % 2) + j:4 * (s % 2) + j + 1],
                                   min_val=0, max_val=caches[0].shape[0] - 1) for j in range(4)]
            if reuse:
                past_used(sp, b, s)
            for j, page in enumerate(pages):
                sp.dma_start(slot[s][:, j * 512:(j + 1) * 512],
                             caches[s // 2][bass.ds(page, 1), :, :].rearrange("n s d -> (n s) d")
                             ).then_inc(page_loaded[s], 16)

        def load_weights(sp, e, s):
            if s < KD:
                src = a["w_gate_up"][0, bass.ds(e, 1), s * P:(s + 1) * P, :].rearrange("e p n -> (e p) n")
                dst = slot[s]
            else:
                j = s - KD
                src = a["w_down"][0, bass.ds(e, 1), 2 * j * P:(2 * j + 2) * P, :].rearrange("e (r p) n -> p (e r) n", p=P)
                dst = slot[s].rearrange("p (r n) -> p r n", r=2)
            sp.dma_start(dst, src).then_inc(w_loaded[s], 16)

        def rev(t, n):
            return t[:, 0:n][:, ::-1]

        def proj_dst(b, n, rows):
            if n in (2, 5):
                return v_new[rows, b, (n // 3) * 512:(n // 3) * 512 + 512]
            i = {0: 0, 1: 1, 3: 2, 4: 3}[n]
            return qk_rows[rows, b, i * 512:i * 512 + 512]

        lam_in = room(4 * HD, at=proj_end)
        lam_tmp = room(4 * HD, at=proj_end + 4 * HD)

        with nc.Block() as block:
            @block.sync
            def _(sp):
                sp.dma_start(ident, consts[:, 0:P]).then_inc(ident_loaded, 16)
                for b in (2, 0, 1):
                    sp.dma_start(x_in[0:BLOCKS[b][1], b, :], x_dram[b]).then_inc(x_loaded[b], 16)
                for k in range(KD):
                    sp.dma_start(ring[:, k * PROJ:(k + 1) * PROJ], w_in[k * P:(k + 1) * P, :]).then_inc(w_sem[k], 16)
                sp.dma_start(tab[:, P:], consts[:, P:]).then_inc(tab_loaded, 16)
                for i, n in enumerate(("lambda_q1", "lambda_k1", "lambda_q2", "lambda_k2")):
                    sp.dma_start(lam_in[:, i * HD:(i + 1) * HD], a[n].to_broadcast([P, HD])).then_inc(lam_loaded, 16)
                for s in range(8):
                    sp.wait_ge(w_in_used, ((s + 1) * SLOT - 1) // PROJ + 1)
                    load_pages(sp, 0, s)

            @block.tensor
            def _(pe):
                done = Count(pe, pe_done)
                evac = {"act": Count(pe, act_done), "dve": Count(pe, dve_done)}
                pe.wait_ge(ident_loaded, 16)
                for n, b in enumerate((2, 0, 1)):
                    t0, nt = BLOCKS[b]
                    pe.wait_ge(x_loaded[b], 16)
                    for g in range(2):
                        if n:
                            evac["act" if g == 0 else "dve"].next()
                        for c in range(4):
                            k = 4 * g + c
                            ins = nc.tensor.transpose(psum[:, 6 + g, c * P:c * P + nt],
                                                      x_in[0:nt, b, k * P:(k + 1) * P], ident[0:nt, 0:nt])
                        done.mark(ins)
                evac["act"].next()
                evac["dve"].next()
                for k in range(KD):
                    pe.wait_ge(w_sem[k], 16)
                    for n in range(3):
                        for h in range(2):
                            col = k * PROJ + (n + 3 * h) * 512
                            ins = nc.tensor.matmul(psum[64 * h:64 * h + 64, n, :], xT[:, k, 256:320],
                                                   ring[:, col:col + 512], start=(k == 0), stop=(k == KD - 1))
                done.mark(ins)
                bank_of = [3, 4, 5, 0, 1, 2]
                for n in range(6):
                    if n == 3:
                        evac["act"].next(3)
                        evac["dve"].next(3)
                    for k in range(KD):
                        col = k * PROJ + n * 512
                        ins = nc.tensor.matmul(psum[:, bank_of[n], :], xT[:, k, 0:128], ring[:, col:col + 512],
                                               start=(k == 0), stop=(k == KD - 1))
                    done.mark(ins)
                for k in range(KD):
                    for n in range(6):
                        if k == 0:
                            evac["act" if n % 2 == 0 else "dve"].next()
                        col = k * PROJ + n * 512
                        ins = nc.tensor.matmul(psum[:, bank_of[n], :], xT[:, k, 128:256], ring[:, col:col + 512],
                                               start=(k == 0), stop=(k == KD - 1))
                    ins.then_inc(w_in_used, 1)
                done.mark(nc.tensor.matmul(psum[:, 7, 0:1], xT[:, 0, 0:128], ident[:, 0:1], start=True, stop=True))
                evac["act"].next(3)
                evac["dve"].next(3)
                for n in range(12):
                    b, i = (2, 0, 1)[n // 4], n % 4
                    nt = BLOCKS[b][1]
                    if n >= 2:
                        evac["act" if n % 2 == 0 else "dve"].next()
                    for h in range(4):
                        ins = nc.tensor.transpose(psum[:, 6 + n % 2, h * P:h * P + nt],
                                                  qk_rows[0:nt, b, i * 512 + h * P:i * 512 + (h + 1) * P],
                                                  ident[0:nt, 0:nt])
                    done.mark(ins)

            def projection_copies(eng, me, own):
                done = Count(eng, pe_done)

                def copy(dst, src, scale=1.0):
                    if me == 0:
                        return nc.scalar.activation(dst, src, ACT.Copy, scale=scale)
                    if scale == 1.0:
                        return nc.vector.tensor_copy(dst, src)
                    return nc.vector.tensor_scalar(dst, src, scale, None, ALU.mult)

                for b in (2, 0, 1):
                    t0, nt = BLOCKS[b]
                    done.next(2)
                    own.mark(copy(xT[:, 4 * me:4 * me + 4, t0:t0 + nt],
                                  psum[:, 6 + me, :].rearrange("p (c t) -> p c t", c=4)[:, :, 0:nt]))
                done.next()
                for n in range(3):
                    own.mark(copy(proj_dst(2, n + 3 * me, slice(0, 64)), psum[64 * me:64 * me + 64, n, :]))
                bank_of = [3, 4, 5, 0, 1, 2]
                for n in range(6):
                    done.next()
                    if n % 2 == me:
                        own.mark(copy(proj_dst(0, n, slice(0, 128)), psum[:, bank_of[n], :]))
                done.next()
                for n in range(6):
                    if n % 2 == me:
                        own.mark(copy(proj_dst(1, n, slice(0, 128)), psum[:, bank_of[n], :]))
                for n in range(12):
                    b, i = (2, 0, 1)[n // 4], n % 4
                    t0, nt = BLOCKS[b]
                    done.next()
                    if n % 2 != me:
                        continue
                    src = psum[:, 6 + n % 2, :].rearrange("p (h t) -> p h t", h=4)[:, :, 0:nt]
                    scale = Q_SCALE if i % 2 == 0 else 1.0
                    if b == 2 and i % 2 == 0:
                        eng.wait_ge(pool_done, 1)
                        for c in range(2):
                            for h in range(4):
                                ins = copy(q_all[64 * c:64 * c + 64, :, i // 2, 32 * h + 8 * c:32 * h + 8 * c + 8],
                                           src[64 * c:64 * c + 64, h, :].rearrange("p (b q) -> p b q", b=DEC_B),
                                           scale)
                        own.mark(ins)
                    else:
                        own.mark(copy(qkT[:, i, :, t0:t0 + nt], src, scale))

            @block.scalar
            def _(act):
                own = Count(act, act_done)
                projection_copies(act, 0, own)

            @block.vector
            def _(dve):
                own = Count(dve, dve_done)
                nc.vector.memset(v_new[64:128, 2, :], 0.0)
                projection_copies(dve, 1, own)
                dve.wait_ge(lam_loaded, 64)
                v = lam_in.rearrange("p (n j) -> p n j", n=4)
                own.link(nc.vector.tensor_tensor(lam_tmp[:, 0:2 * HD].rearrange("p (n j) -> p n j", n=2),
                                                 v[:, 0:4:2, :], v[:, 1:4:2, :], ALU.mult))
                own.mark(nc.vector.tensor_reduce(lam_cols[:, 0:2],
                                                 lam_tmp[:, 0:2 * HD].rearrange("p (n j) -> p n j", n=2),
                                                 AX.X, ALU.add))

            @block.gpsimd
            def _(pool):
                nc.gpsimd.memset(q_all, 0.0).then_inc(pool_done, 1)
                dsts = {1: "sb_k", 2: "sb_v", 4: "diff_k", 5: "diff_v"}
                acts, dves = Count(pool, act_done), Count(pool, dve_done)
                acts.n, dves.n = 3, 3
                for b in (2, 0, 1):
                    acts.next(3)
                    dves.next(3)
                    for n, what in dsts.items():
                        pool.dma_start(out[(what, b)], proj_dst(b, n, slice(0, BLOCKS[b][1]))).then_inc(rows_out, 16)
                pool.wait_ge(rows_out, 12 * 16)
        NK = PAST + SAMPLES
        NKP = PAST + P
        NCH = NKP // P
        top[0] = att_at
        kT = [room(4 * 512).rearrange("p (h k) -> p h k", h=4) for _ in range(2)]
        soft, stick, prob = room(NKP), room(NKP), room(NKP)
        wT = [room(NCH * P).rearrange("p (k r) -> p k r", k=NCH) for _ in range(2)]
        q_now = room(2 * P).rearrange("p (y r) -> p y r", y=2)
        o_rows = [room(P) for _ in range(2)]
        o_tmp = room(32).rearrange("p (h q) -> p h q", h=4)
        zeros = room(D)
        cols = room(64)
        one, neg_max, total, factor, coef, neg_lam, lam_e = (
            cols[:, 0:1], cols[:, 1:9], cols[:, 9:17], cols[:, 17:25], cols[:, 25:26], cols[:, 26:27], cols[:, 27:29])
        Z = [psum[:, 0:2, :].rearrange("p b c -> p (b c)"), psum[:, 2:4, :].rearrange("p b c -> p (b c)")]
        BY_KIND = (4, 7)
        ZN = [psum[:, n, 0:64] for n in BY_KIND]
        O = [psum[:, n, 128:256] for n in BY_KIND]
        OT = [psum[:, n, 256:384] for n in BY_KIND]
        copied = {"dve": sem("copied_dve"), "act": sem("copied_act")}
        scored = sem("scored")
        z_ready = [sem("z_sb_ready"), sem("z_diff_ready")]
        q_ready = sem("q_ready")
        log_ready = sem("log_ready")
        stick_ready = sem("stick_ready")
        w_ready = [sem("w_sb_ready"), sem("w_diff_ready")]
        max_ready = sem("max_ready")
        factor_ready = sem("factor_ready")
        mixed = [sem("mixed_sb"), sem("mixed_diff")]
        o_copied = sem("o_copied")
        o_turned = [sem("o_sb_turned"), sem("o_diff_turned")]
        mix_stored = sem("mix_stored")
        setup_done, rows_zeroed = sem("setup_done"), sem("rows_zeroed")
        who = lambda j: "dve" if j % 2 == 0 else "act"
        units = [(0, 0, 0, 8), (1, 0, 0, 8), (0, 1, 0, 4), (1, 1, 0, 4), (0, 1, 4, 4), (1, 1, 4, 4)]

        def place(nh, h):
            return (h % 2) * (nh // 2) + h // 2

        p_scored, p_turned, p_copied = sem("prompt_scored"), sem("prompt_turned"), sem("prompt_copied")
        p_log, p_stick, p_w = sem("prompt_log"), sem("prompt_stick"), [sem("prompt_sb_weights"), sem("prompt_diff_weights")]
        p_exp, mix_part = sem("prompt_exp"), sem("mix_part")
        p_max, p_mixed, p_stored = sem("prompt_max"), sem("prompt_mixed"), sem("prompt_stored")
        p_free = sem("prompt_scores_used")

        with nc.Block() as block:
            def copy_bank(eng, b, j):
                eng.wait_ge(turned, b * TURNS + (j + 1))
                src = psum[:, 5 + j % 2, :]
                if j < 16:
                    y, pg = j // 8, j % 8
                    eng.wait_ge(scored, 4 * b + (pg // 4 + 1) * y + SEED)
                    dst, src = kT[pg // 4][:, :, (pg % 4) * P:(pg % 4 + 1) * P], src.rearrange("p (h k) -> p h k", h=4)
                else:
                    y, n = (j - 16) // 3, (j - 16) % 3
                    k0, k1 = 4 * n, min(4 * n + 4, NCH)
                    eng.wait_ge(mixed[y], b + SEED)
                    dst, src = wT[y][:, k0:k1, :], src.rearrange("p (k r) -> p k r", k=4)[:, 0:k1 - k0, :]
                if who(j) == "dve":
                    nc.vector.tensor_copy(dst, src).then_inc(copied["dve"], 1)
                else:
                    nc.scalar.activation(dst, src, ACT.Copy).then_inc(copied["act"], 1)

            @block.sync
            def _(sp):
                for j in range(4):
                    sp.dma_start(slot[8 + j].rearrange("p (r n) -> p r n", r=2),
                                 a["w_out"][0, 2 * j * P:(2 * j + 2) * P, :].rearrange("(r p) n -> p r n", p=P)
                                 ).then_inc(w_out_loaded, 16)
                with sp.Fori(1, DEC_B) as b:
                    for s in (0, 1, 2, 3, 4, 5, 6, 7):
                        load_pages(sp, b, s, True)
                for s in range(8):
                    past_used(sp, DEC_B, s)
                    load_weights(sp, 0, s)

            @block.gpsimd
            def _(pool):
                nc.gpsimd.memset(prob[:, NK:], 0.0).then_inc(pool_done, 1)
                nc.gpsimd.memset(zeros, 0.0).then_inc(pool_done, 1)
                pool.wait_ge(pool_done, 3)
                pool.dma_start(y_dram[EXPERTS * SLOTS:, :].rearrange("(i s) d -> s i d", s=SLOTS),
                               zeros[0:SLOTS, :].rearrange("p (o d) -> p o d", o=1).to_broadcast([SLOTS, MAX_EXTRA, D])
                               ).then_inc(rows_zeroed, 16)
                with pool.Fori(0, DEC_B) as b:
                    pool.wait_ge(z_ready[1], b + SEED)
                    nc.gpsimd.tensor_copy(q_now, q_all[:, bass.ds(b, 1), :, :].rearrange("p b y r -> p (b y) r")
                                          ).then_inc(q_ready, 1)
                pool.wait_ge(rows_zeroed, 16)

            @block.tensor
            def _(pe):
                for s in (*z_ready, scored, *mixed, *o_turned):
                    pe.sem_inc(s, SEED)
                with pe.Fori(0, DEC_B) as b:
                    ev = lambda j: (copied[who(j)], b * (TURNS // 2) + (j // 2 + 1 + SEED))

                    def bank_free(j):
                        if j >= 2:
                            pe.wait_ge(*ev(j - 2))
                        else:
                            pe.wait_ge(copied[who(j)], b * (TURNS // 2) + SEED)

                    for y in range(2):
                        for pg in range(PAGES):
                            j = 8 * y + pg
                            s = 2 * y + pg // 4
                            if pg % 4 == 0:
                                pe.wait_ge(page_loaded[s], 64 * b + 64)
                            bank_free(j)
                            for h in range(4):
                                at = (pg % 4) * 512 + h * P
                                ins = nc.tensor.transpose(psum[:, 5 + j % 2, h * P:(h + 1) * P],
                                                          slot[s][:, at:at + P], ident)
                            ins.then_inc(turned, 1)
                        if y == 0:
                            pe.wait_ge(q_ready, b + 1)
                            pe.wait_ge(stick_ready, 2 * b + SEED)
                        else:
                            pe.wait_ge(max_ready, b + SEED)
                        for c in range(2):
                            pe.wait_ge(*ev(8 * y + 4 * c + 2))
                            pe.wait_ge(*ev(8 * y + 4 * c + 3))
                            for h in range(4):
                                ins = nc.tensor.matmul(Z[y][32 * h:32 * h + 32, c * 512:(c + 1) * 512],
                                                       q_now[:, y, 32 * h:32 * h + 32], kT[c][:, h, :],
                                                       start=True, stop=True)
                            ins.then_inc(scored, 1)
                        pe.wait_ge(mix_stored, 2 * b + SEED)
                        for h in range(4):
                            ins = nc.tensor.matmul(ZN[y][32 * h:32 * h + 32, :], q_now[:, y, 32 * h:32 * h + 32],
                                                   qkT[:, 2 * y + 1, h, 256:320], start=True, stop=True)
                        ins.then_inc(z_ready[y], 1)
                    for y in range(2):
                        pe.wait_ge(w_ready[y], b + 1)
                        for n in range(3):
                            j = 16 + 3 * y + n
                            bank_free(j)
                            chunks = range(4 * n, min(4 * n + 4, NCH))
                            for k in chunks:
                                ins = nc.tensor.transpose(psum[:, 5 + j % 2, (k % 4) * P:(k % 4 + 1) * P],
                                                          (stick if y == 0 else prob)[:, k * P:(k + 1) * P], ident)
                            ins.then_inc(turned, 1)
                        for k in range(NCH):
                            if k % 4 == 0:
                                pe.wait_ge(*ev(16 + 3 * y + k // 4))
                                if k < 8:
                                    pe.wait_ge(page_loaded[4 + 2 * y + k // 4], 64 * b + 64)
                            for h in range(4):
                                if k < 8:
                                    v = slot[4 + 2 * y + k // 4][:, (k % 4) * 512 + h * P:(k % 4) * 512 + (h + 1) * P]
                                else:
                                    v = v_new[:, 2, y * 512 + h * P:y * 512 + (h + 1) * P]
                                ins = nc.tensor.matmul(O[y][32 * h:32 * h + 32, :], wT[y][:, k, 32 * h:32 * h + 32],
                                                       v, start=(k == 0), stop=(k == NCH - 1))
                            if k in (3, 7):
                                ins.then_inc(slot_used[4 + 2 * y + k // 4], 1)
                        ins.then_inc(mixed[y], 1)
                    for y in range(2):
                        pe.wait_ge(o_copied, 2 * b + y + 1)
                        nc.tensor.transpose(OT[y], o_rows[y], ident).then_inc(o_turned[y], 1)
                ztile = lambda u: Z[u % 2]

                def score(u):
                    y, qb, h0, nh = units[u]
                    width = 128 * (qb + 1)
                    if u >= 2:
                        pe.wait_ge(p_free, u - 1)
                    for h in range(nh):
                        hh, at = h0 + h, place(nh, h) * width
                        r = slice(64 * (hh % 2), 64 * (hh % 2) + 64)
                        ins = nc.tensor.matmul(ztile(u)[:, at:at + width],
                                               qkT[r, 2 * y, hh // 2, qb * P:(qb + 1) * P],
                                               qkT[r, 2 * y + 1, hh // 2, 0:width], start=True, stop=True)
                    ins.then_inc(p_scored, 1)

                turns = [0]

                def mix(u):
                    y, qb, h0, nh = units[u]
                    nkb = qb + 1
                    pe.wait_ge(p_w[y], u // 2 + 1)
                    for g in range(2 - y):
                        t = turns[0]
                        if t >= 2:
                            pe.wait_ge(p_copied, t - 1)
                        for c in range(4):
                            ins = nc.tensor.transpose(psum[:, 5 + t % 2, c * P:(c + 1) * P],
                                                      (stick if y == 0 else prob)[:, (4 * g + c) * P:(4 * g + c + 1) * P],
                                                      ident)
                        ins.then_inc(p_turned, 1)
                        turns[0] += 1
                    pe.wait_ge(p_copied, turns[0])
                    if y == 0 and u > 0 and h0 == 0:
                        pe.wait_ge(p_stored, 1)
                    if y == 1 and u > 1 and h0 == 0:
                        pe.wait_ge(p_stored, 2)
                    n_out = nh // (1 + y)
                    for h in range(n_out):
                        hh = h0 // (1 + y) + h
                        for kb in range(nkb):
                            if y == 0:
                                dst = psum[64 * (hh % 2):64 * (hh % 2) + 64, 4, (hh // 2) * P:(hh // 2 + 1) * P]
                                v = v_new[:, kb, hh * HD:(hh + 1) * HD]
                            else:
                                dst = psum[:, 7, hh * P:(hh + 1) * P]
                                v = v_new[:, kb, 512 + hh * P:512 + (hh + 1) * P]
                            ins = nc.tensor.matmul(dst, v, wT[y][:, (place(nh, h) if y == 0 else h) * nkb + kb, :],
                                                   start=(kb == 0), stop=(kb == nkb - 1))
                    ins.then_inc(p_mixed, 1)

                pe.wait_ge(stick_ready, 2 * DEC_B + SEED)
                score(0)
                pe.wait_ge(max_ready, DEC_B + SEED)
                pe.wait_ge(copied["act"], DEC_B * TURNS // 2 + SEED)
                pe.wait_ge(copied["dve"], DEC_B * TURNS // 2 + SEED)
                pe.wait_ge(mix_stored, 2 * DEC_B + SEED)
                score(1)
                for u in range(6):
                    mix(u)
                    if u + 2 < 6:
                        score(u + 2)

            @block.scalar
            def _(act):
                own = Count(act, act_own)
                act.sem_inc(copied["act"], SEED)
                nc.scalar.activation(lam_e, lam_cols[:, 0:2], ACT.Exp).then_inc(setup_done, 1)
                with act.Fori(0, DEC_B) as b:
                    own.enter(b, 3)

                    def bank(j):
                        copy_bank(act, b, j)

                    for j in (1, 3, 5, 7):
                        bank(j)
                    act.wait_ge(z_ready[0], b + 1 + SEED)
                    own.mark(nc.scalar.activation(soft[:, 0:PAST], Z[0], ACT.Abs))
                    own.link(nc.scalar.activation(soft[:, PAST:NK], ZN[0], ACT.Abs))
                    bank(9)
                    own.link(nc.scalar.activation(soft[:, 0:NK], soft[:, 0:NK], ACT.Exp, scale=-1.0))
                    bank(11)
                    nc.scalar.activation(soft[:, 0:NK], soft[:, 0:NK], ACT.Ln, bias=1.0).then_inc(log_ready, 1)
                    bank(13)
                    bank(15)
                    act.wait_ge(stick_ready, 2 * b + 2 + SEED)
                    nc.scalar.activation(stick[:, 0:NK], stick[:, 0:NK], ACT.Exp).then_inc(w_ready[0], 1)
                    act.wait_ge(max_ready, b + 1 + SEED)
                    nc.scalar.activation(prob[:, 0:NK], prob[:, 0:NK], ACT.Exp, bias=neg_max[:, 0:1],
                                         accum_out=total[:, 0:1]).then_inc(w_ready[1], 1)
                    bank(17)
                    bank(19)
                    act.wait_ge(mixed[0], b + 1 + SEED)
                    act.wait_ge(o_turned[0], b + SEED)
                    nc.scalar.activation(o_rows[0], O[0], ACT.Copy).then_inc(o_copied, 1)
                    bank(21)
                    act.wait_ge(mixed[1], b + 1 + SEED)
                    act.wait_ge(o_turned[1], b + SEED)
                    act.wait_ge(factor_ready, b + 1)
                    nc.scalar.activation(o_rows[1], O[1], ACT.Copy, scale=factor[:, 0:1]).then_inc(o_copied, 1)
                    own.leave(DEC_B)
                for u, (y, qb, h0, nh) in enumerate(units):
                    width = 128 * (qb + 1)
                    if y == 0:
                        act.wait_ge(p_scored, u + 1)
                        own.link(nc.scalar.activation(soft[:, 0:PAST], Z[u % 2], ACT.Abs))
                        own.link(nc.scalar.activation(soft[:, 0:PAST], soft[:, 0:PAST], ACT.Exp, scale=-1.0))
                        nc.scalar.activation(soft[:, 0:PAST], soft[:, 0:PAST], ACT.Ln, bias=1.0).then_inc(p_log, 1)
                        act.wait_ge(p_stick, u // 2 + 1)
                        nc.scalar.activation(stick[:, 0:PAST], stick[:, 0:PAST], ACT.Exp).then_inc(p_w[y], 1)
                    else:
                        act.wait_ge(p_max, u // 2 + 1)
                        for h in range(nh):
                            own.mark(nc.scalar.activation(prob[:, h * width:(h + 1) * width],
                                                          prob[:, h * width:(h + 1) * width], ACT.Exp,
                                                          bias=neg_max[:, h:h + 1], accum_out=total[:, h:h + 1]))
                        own.wait()
                        act.nop().then_inc(p_exp, 1)

            @block.vector
            def _(dve):
                own = Count(dve, dve_own)
                for s in (copied["dve"], stick_ready, max_ready, mix_stored):
                    dve.sem_inc(s, SEED)
                own.mark(nc.vector.memset(one, 1.0))
                own.mark(nc.vector.memset(stick[:, NK:], 0.0))
                dve.wait_ge(setup_done, 1)
                own.link(nc.vector.tensor_tensor(neg_lam, lam_e[:, 1:2], lam_e[:, 0:1], ALU.subtract))
                own.link(nc.vector.tensor_scalar(neg_lam, neg_lam, -LAM_INIT, None, ALU.add))
                own.link(nc.vector.scalar_tensor_tensor(out=coef, in0=const["is_c1"], scalar=neg_lam,
                                                        in1=const["is_c0"], op0=ALU.mult, op1=ALU.add))
                dve.wait_ge(tab_loaded, 16)
                with dve.Fori(0, DEC_B) as b:
                    own.enter(b, 9)
                    own_keys = lambda n: const[n][:, bass.ds(56 - 8 * b, SAMPLES)]

                    def bank(j):
                        copy_bank(dve, b, j)

                    for j in (0, 2, 4, 6, 8, 10):
                        bank(j)
                    dve.wait_ge(log_ready, b + 1)
                    own.mark(nc.vector.scalar_tensor_tensor(out=soft[:, 0:PAST], in0=Z[0], scalar=0.0,
                                                            in1=soft[:, 0:PAST], op0=ALU.max, op1=ALU.add))
                    own.link(nc.vector.scalar_tensor_tensor(out=soft[:, PAST:NK], in0=ZN[0], scalar=0.0,
                                                            in1=soft[:, PAST:NK], op0=ALU.max, op1=ALU.add))
                    own.link(nc.vector.tensor_tensor(soft[:, PAST:NK], soft[:, PAST:NK], own_keys("nmask"), ALU.mult))
                    own.link(nc.vector.tensor_tensor_scan(out=rev(stick, NK),
                                                          data0=one.to_broadcast([P, NK]), data1=rev(soft, NK),
                                                          initial=0.0, op0=ALU.mult, op1=ALU.add))
                    nc.vector.tensor_tensor(stick[:, 0:PAST], Z[0], stick[:, 0:PAST], ALU.subtract
                                            ).then_inc(stick_ready, 1)
                    own.link(nc.vector.tensor_tensor(stick[:, PAST:NK], ZN[0], stick[:, PAST:NK], ALU.subtract))
                    nc.vector.tensor_tensor(stick[:, PAST:NK], stick[:, PAST:NK], own_keys("nneg"), ALU.add
                                            ).then_inc(stick_ready, 1)
                    bank(12)
                    bank(14)
                    dve.wait_ge(z_ready[1], b + 1 + SEED)
                    own.mark(nc.vector.tensor_tensor(prob[:, 0:PAST], Z[1], const["sbias"], ALU.add))
                    own.link(nc.vector.tensor_tensor(prob[:, PAST:NK], ZN[1], own_keys("nbias"), ALU.add))
                    own.link(nc.vector.tensor_reduce(neg_max[:, 1:2], prob[:, 0:NK], AX.X, ALU.max))
                    nc.vector.tensor_scalar(neg_max[:, 0:1], neg_max[:, 1:2], -1.0, None, ALU.mult
                                            ).then_inc(max_ready, 1)
                    bank(16)
                    bank(18)
                    dve.wait_ge(w_ready[1], b + 1)
                    own.link(nc.vector.reciprocal(factor[:, 1:2], total[:, 0:1]))
                    nc.vector.tensor_tensor(factor[:, 0:1], factor[:, 1:2], coef, ALU.mult).then_inc(factor_ready, 1)
                    bank(20)
                    tok = bass.ds(PROMPT + 8 * b, DEC_T)
                    dve.wait_ge(o_turned[0], b + 1 + SEED)
                    t = OT[0].rearrange("p (h r) -> p h r", h=4)
                    nc.vector.tensor_copy(mixT[0:64, 0:4, tok], t[0:64, :, 0:8]).then_inc(mix_part, 1)
                    nc.vector.tensor_copy(mixT[64:128, 0:4, tok], t[64:128, :, 8:16]).then_inc(mix_stored, 1)
                    dve.wait_ge(o_turned[1], b + 1 + SEED)
                    t = OT[1].rearrange("p (h r) -> p h r", h=4)
                    nc.vector.tensor_copy(o_tmp, t[:, :, 0:8]).then_inc(mix_part, 1)
                    dve.wait_ge(mix_part, 2 * b + 2)
                    nc.vector.tensor_tensor(mixT[:, 4:8, tok], t[:, :, 8:16], o_tmp, ALU.add).then_inc(mix_stored, 1)
                    own.leave(DEC_B)
                pturn = 0
                pending = None

                def store(u):
                    y, qb, h0, nh = units[u]
                    dve.wait_ge(p_mixed, u + 1)
                    nc.vector.tensor_copy(mixT[:, 4 * y:4 * y + 4, qb * P:(qb + 1) * P],
                                          psum[:, 7 if y else 4, :].rearrange("p (h q) -> p h q", h=4)
                                          ).then_inc(p_stored, 1)

                for u, (y, qb, h0, nh) in enumerate(units):
                    width = 128 * (qb + 1)
                    heads = lambda t: t[:, 0:PAST].rearrange("p (h k) -> p h k", h=nh)
                    tile = lambda n: const[n][:, 256 - width:256]
                    if y == 0:
                        over = lambda n: tile(n).rearrange("p (o k) -> p o k", o=1).to_broadcast([P, nh, width])
                        dve.wait_ge(p_log, u // 2 + 1)
                        own.link(nc.vector.scalar_tensor_tensor(out=soft[:, 0:PAST], in0=Z[u % 2], scalar=0.0,
                                                                in1=soft[:, 0:PAST], op0=ALU.max, op1=ALU.add))
                        own.link(nc.vector.tensor_tensor(heads(soft), heads(soft), over("pmask"), ALU.mult))
                        for h in range(nh):
                            seg = slice(h * width, (h + 1) * width)
                            own.mark(nc.vector.tensor_tensor_scan(
                                out=rev(stick[:, seg], width), data0=one.to_broadcast([P, width]),
                                data1=rev(soft[:, seg], width), initial=0.0, op0=ALU.mult, op1=ALU.add))
                        own.wait()
                        nc.vector.tensor_tensor(stick[:, 0:PAST], Z[u % 2], stick[:, 0:PAST], ALU.subtract
                                                ).then_inc(p_free, 1)
                        dve.wait_ge(p_free, u + 1)
                        nc.vector.tensor_tensor(heads(stick), heads(stick), over("pneg"), ALU.add
                                                ).then_inc(p_stick, 1)
                    else:
                        dve.wait_ge(p_scored, u + 1)
                        both = lambda t, h: t[:, 0:PAST].rearrange("p (c k) -> p c k", c=2)[:, :, h * width:(h + 1) * width]
                        for h in range(nh // 2):
                            ins = nc.vector.scalar_tensor_tensor(
                                out=both(prob, h),
                                in0=tile("pdist").rearrange("p (o k) -> p o k", o=1).to_broadcast([P, 2, width]),
                                scalar=SLOPES[h0 // 2 + h], in1=both(Z[u % 2], h), op0=ALU.mult, op1=ALU.add)
                            if h < nh // 2 - 1:
                                own.mark(ins)
                        ins.then_inc(p_free, 1)
                        own.wait()
                        dve.wait_ge(p_free, u + 1)
                        own.link(nc.vector.tensor_reduce(factor[:, 0:nh], heads(prob), AX.X, ALU.max))
                        nc.vector.tensor_scalar(neg_max[:, 0:nh], factor[:, 0:nh], -1.0, None, ALU.mult
                                                ).then_inc(p_max, 1)
                        dve.wait_ge(p_exp, u // 2 + 1)
                        own.link(nc.vector.reciprocal(factor[:, 0:nh], total[:, 0:nh]))
                        own.link(nc.vector.tensor_scalar(factor[:, nh // 2:nh], factor[:, nh // 2:nh], neg_lam, None, ALU.mult))
                        for h in range(nh // 2):
                            s0 = slice(h * width, (h + 1) * width)
                            s1 = slice(512 + h * width, 512 + (h + 1) * width)
                            own.link(nc.vector.tensor_scalar(prob[:, s0], prob[:, s0], factor[:, h:h + 1],
                                                             None, ALU.mult))
                            own.link(nc.vector.scalar_tensor_tensor(
                                out=prob[:, s0], in0=prob[:, s1], scalar=factor[:, nh // 2 + h:nh // 2 + h + 1],
                                in1=prob[:, s0], op0=ALU.mult, op1=ALU.add))
                        dve.nop().then_inc(p_w[y], 1)
                    if u in (2, 3):
                        store(u - 2)
                    for g in range(2 - y):
                        pturn += 1
                        if u >= 2:
                            dve.wait_ge(p_mixed, u - 1)
                        dve.wait_ge(p_turned, pturn)
                        nc.vector.tensor_copy(wT[y][:, 4 * g:4 * g + 4, :],
                                              psum[:, 5 + (pturn - 1) % 2, :].rearrange("p (k r) -> p k r", k=4)
                                              ).then_inc(p_copied, 1)
                store(4)
                store(5)

        top[0] = after_mix
        x1 = room(3 * D).rearrange("p (b d) -> p b d", b=3)
        base = room(3 * D).rearrange("p (b d) -> p b d", b=3)
        gates = room(12).rearrange("p (b k) -> p b k", b=3)
        norm_cols = room(64)
        ln_rows = room(4 * D).rearrange("p (n d) -> p n d", n=4)
        kept_end = top[0]
        x_again = room(3 * D).rearrange("p (b d) -> p b d", b=3)
        res = room(2 * D).rearrange("p (n d) -> p n d", n=2)
        x1T = room(KD * TOKENS).rearrange("p (k t) -> p k t", k=KD)
        w_route = room(KD * EXPERTS).rearrange("p (k e) -> p k e", k=KD)
        b_route = room(EXPERTS)
        b_down = room(D)
        gain = room(2)
        ones = room(P)
        top8 = room(3 * 8).rearrange("p (b k) -> p b k", b=3)
        which = room(3 * 4).rearrange("p (b k) -> p b k", b=3)
        logits = room(EXPERTS)
        hot = room(12 * EXPERTS).rearrange("p (b k e) -> p b k e", b=3, k=TOP_K)
        picked = room(3 * EXPERTS).rearrange("p (b e) -> p b e", b=3)
        weight = room(3 * EXPERTS).rearrange("p (b e) -> p b e", b=3)
        weightT = room(3 * P).rearrange("p (b t) -> p b t", b=3)
        rank = room(4 * EXPERTS).rearrange("p (b e) -> p b e", b=4)
        work = [room(4 * EXPERTS).rearrange("p (b e) -> p b e", b=4) for _ in range(6)]
        hot_tmp = room(4 * EXPERTS).rearrange("p (k e) -> p k e", k=4)
        places = room(24).rearrange("p (n j) -> p n j", n=2)
        extra_col = room(2)
        assert top[0] <= 52800
        squares, r_norm = x1T.rearrange("p k t -> p (k t)")[:, 0:4 * TOKENS], x1T.rearrange("p k t -> p (k t)")[:, 4 * TOKENS:]
        diffT = mixT[:, 4:8, :].rearrange("p h t -> p (h t)")

        idx_all = small_i[:, 0:64]
        place_y, place_t = small_i[:, 64:76], small_i[:, 76:88]
        token2_i, extra_i, count_i = small_i[:, 88:91], small_i[:, 91:92], small_i[:, 92:93]
        zero_i, idx_now = small_i[:, 96:160], small_i[:, 160:161]
        idx8 = small_i[:, 168:192].bitcast(U32).rearrange("p (b k) -> p b k", b=3)

        c_loaded = sem("c_loaded")
        x_again_loaded = [sem(f"x_again_loaded{b}") for b in range(3)]
        o_pe, o_act, o_dve = sem("o_pe"), sem("o_act"), sem("o_dve")
        ln_loaded = sem("ln_loaded")
        x1_stored, zeroed, placed, table_loaded, extra_stored = (
            sem("x1_stored"), sem("table_zeroed"), sem("tokens_placed"), sem("table_loaded"), sem("extra_stored"))
        places_ready, idx_ready, x1_ready = sem("places_ready"), sem("idx_ready"), sem("x1_ready")
        order = (2, 0, 1)
        half_moved, root_ready, var_ready, std_ready, eps_ready = (
            sem("half_moved"), sem("root_ready"), sem("var_ready"), sem("std_ready"), sem("eps_ready"))
        top_ready, gate_ready, logits_read, picked_ready, weight_ready, base_ready, extra_ready = (
            sem("top_ready"), sem("gate_ready"), sem("logits_read"), sem("picked_ready"), sem("weight_ready"),
            sem("base_ready"), sem("extra_ready"))
        dve_link, f_link = sem("dve_link"), sem("final_link")
        one_col = ones[:, 0:1]

        def norm(dve, link, r, nt, n, dst, g, ready, loaded):
            m = n % 3
            stats = norm_cols[0:nt, 36:48].rearrange("p (c s) -> p c s", c=2)
            for c in range(2):
                link.mark(nc.vector.bn_stats(stats[:, c, :], r[:, c * 512:(c + 1) * 512]))
            link.wait()
            mean, var = norm_cols[0:nt, 8 + 2 * m:9 + 2 * m], norm_cols[0:nt, 9 + 2 * m:10 + 2 * m]
            nc.vector.bn_aggr(norm_cols[0:nt, 8 + 2 * m:10 + 2 * m], stats).then_inc(var_ready, 1)
            dve.wait_ge(std_ready, n + 1)
            root = norm_cols[0:nt, 16 + n:17 + n]
            link.link(nc.vector.reciprocal(root, root))
            link.link(nc.vector.tensor_scalar(r, r, mean, root, ALU.subtract, ALU.mult))
            if loaded is not None:
                dve.wait_ge(loaded, 64)
            link.link(nc.vector.tensor_tensor(r, r, ln_rows[0:nt, g, :], ALU.mult))
            nc.vector.tensor_tensor(dst, r, ln_rows[0:nt, g + 1, :], ALU.add).then_inc(ready, 1)


        with nc.Block() as block:
            @block.sync
            def _(sp):
                for b in order:
                    sp.dma_start(x_again[0:BLOCKS[b][1], b, :], x_dram[b]).then_inc(x_again_loaded[b], 16)
                sp.dma_start(gain[:, 0:1], a["subln_g"].rearrange("o d -> d o")).then_inc(c_loaded, 16)
                sp.dma_start(w_route, a["w_router"][0].rearrange("(k p) e -> p k e", p=P)).then_inc(c_loaded, 16)
                sp.dma_start(b_route, a["b_router"].to_broadcast([P, EXPERTS])).then_inc(c_loaded, 16)
                sp.dma_start(b_down[0:EXPERTS, :], a["b_down"][0]).then_inc(c_loaded, 16)
                for i, n in enumerate(("ln1_g", "ln1_b", "ln2_g", "ln2_b")):
                    sp.dma_start(ln_rows[:, i, :], a[n].to_broadcast([P, D])).then_inc(ln_loaded, 16)
                for s in range(8, RING):
                    sp.wait_ge(o_pe, 4)
                    load_weights(sp, 0, s)
                for n, b in enumerate(order):
                    sp.wait_ge(x1_ready, n + 1)
                    t0, nt = BLOCKS[b]
                    sp.dma_start(x1_dram[2 * t0:2 * (t0 + nt), :].rearrange("(t h) d -> t (h d)", h=2),
                                 x1[0:nt, b, :]).then_inc(x1_stored, 16)

            @block.tensor
            def _(pe):
                pe_o, act_o, dve_o = Count(pe, o_pe), Count(pe, o_act), Count(pe, o_dve)
                dve_o.next(2)
                for n in range(3):
                    w = min(BANK, 4 * TOKENS - n * BANK)
                    ins = nc.tensor.matmul(psum[:, n, 0:w], ones, squares[:, n * BANK:n * BANK + w],
                                           start=True, stop=True)
                pe_o.mark(ins)
                dve_o.next()
                pe.wait_ge(w_out_loaded, 64)
                w_of = lambda k, n: slot[8 + k // 2][:, (k % 2) * D + n * 512:(k % 2) * D + n * 512 + 512]
                for k in range(KD):
                    for h in range(2):
                        ins = nc.tensor.matmul(psum[64 * h:64 * h + 64, 3, :], mixT[:, k, 256:320], w_of(k, h),
                                               start=(k == 0), stop=(k == KD - 1))
                pe_o.mark(ins)
                for b in range(2):
                    for n in range(2):
                        for k in range(KD):
                            ins = nc.tensor.matmul(psum[:, 4 + n if b == 0 else n, :], mixT[:, k, b * P:(b + 1) * P],
                                                   w_of(k, n), start=(k == 0), stop=(k == KD - 1))
                    pe_o.mark(ins)
                pe.wait_ge(c_loaded, 64)
                for n, b in enumerate(order):
                    t0, nt = BLOCKS[b]
                    pe.wait_ge(x1_ready, n + 1)
                    for g in range(2):
                        if n:
                            act_o.wait()
                        for c in range(4):
                            k = 4 * g + c
                            ins = nc.tensor.transpose(psum[:, 6 + g, c * P:c * P + nt], x1[0:nt, b, k * P:(k + 1) * P],
                                                      ident[0:nt, 0:nt])
                    pe_o.mark(ins)
                    act_o.next(2)
                    if n:
                        pe.wait_ge(logits_read, n)
                    for k in range(KD):
                        ins = nc.tensor.matmul(psum[0:nt, 2, 0:EXPERTS], x1T[:, k, t0:t0 + nt], w_route[:, k, :],
                                               start=(k == 0), stop=(k == KD - 1))
                    pe_o.mark(ins)
                pe.wait_ge(picked_ready, 3)
                for b in range(4):
                    for c in range(min(b + 1, 3)):
                        nt = BLOCKS[c][1]
                        ins = nc.tensor.matmul(psum[:, 3, b * EXPERTS:(b + 1) * EXPERTS],
                                               const["before"][0:nt, :] if c == b else ones[0:nt, :],
                                               picked[0:nt, c, :], start=(c == 0), stop=(c == min(b, 2)))
                pe_o.mark(ins)
                pe.wait_ge(weight_ready, 3)
                for b in range(3):
                    nt = BLOCKS[b][1]
                    ins = nc.tensor.transpose(psum[0:EXPERTS, 2, b * P:b * P + nt], weight[0:nt, b, :],
                                              ident[0:nt, 0:nt])
                pe_o.mark(ins)
                act_o.next()
                for i, b in enumerate((0, 1, 2)):
                    nt = BLOCKS[b][1]
                    if b == 2:
                        pe.wait_ge(base_ready, 1)
                    for n in range(2):
                        bank = (4, 5, 6, 7, 4, 5)[2 * i + n]
                        ins = nc.tensor.matmul(psum[0:nt, bank, :], weightT[0:EXPERTS, b, 0:nt],
                                               b_down[0:EXPERTS, n * 512:(n + 1) * 512], start=True, stop=True)
                    pe_o.mark(ins)

            @block.scalar
            def _(act):
                own, pe_o, dve_o = Count(act, o_act), Count(act, o_pe), Count(act, o_dve)
                pe_o.next()
                act.wait_ge(eps_ready, 1)
                for n in range(3):
                    w = min(BANK, 4 * TOKENS - n * BANK)
                    ins = nc.scalar.activation(r_norm[:, n * BANK:n * BANK + w], psum[:, n, 0:w], ACT.Sqrt,
                                               scale=1.0 / P, bias=norm_cols[:, 0:1])
                    ins.then_inc(root_ready, 1)
                pe_o.next()
                nc.scalar.activation(res[0:64, 0, 512:1024], psum[64:128, 3, :], ACT.Copy).then_inc(half_moved, 1)
                for n, b in enumerate(order):
                    act.wait_ge(var_ready, n + 1)
                    nt = BLOCKS[b][1]
                    nc.scalar.activation(norm_cols[0:nt, 16 + n:17 + n], norm_cols[0:nt, 9 + 2 * n:10 + 2 * n], ACT.Sqrt,
                                         bias=norm_cols[0:nt, 0:1]).then_inc(std_ready, 1)
                pe_o.n = 4
                for n, b in enumerate(order):
                    t0, nt = BLOCKS[b]
                    pe_o.next()
                    for g in range(2):
                        own.mark(nc.scalar.activation(x1T[:, 4 * g:4 * g + 4, t0:t0 + nt],
                                                      psum[:, 6 + g, :].rearrange("p (c t) -> p c t", c=4)[:, :, 0:nt],
                                                      ACT.Copy))
                    pe_o.n += 1
                for n, b in enumerate(order):
                    nt = BLOCKS[b][1]
                    act.wait_ge(top_ready, n + 1)
                    nc.scalar.activation(gates[0:nt, b, :], top8[0:nt, b, 0:TOP_K], ACT.Exp,
                                         bias=norm_cols[0:nt, 24 + b:25 + b],
                                         accum_out=norm_cols[0:nt, 28 + b:29 + b]).then_inc(gate_ready, 1)
                pe_o.n = 11
                pe_o.next()
                for b in range(3):
                    nt = BLOCKS[b][1]
                    ins = nc.scalar.activation(weightT[0:EXPERTS, b, 0:nt], psum[0:EXPERTS, 2, b * P:b * P + nt], ACT.Copy)
                own.mark(ins)

            @block.vector
            def _(dve):
                own, link = Count(dve, o_dve), Count(dve, dve_link)
                link.mark(nc.vector.tensor_tensor(squares, diffT, diffT, ALU.mult))
                nc.vector.memset(norm_cols[:, 0:1], EPS).then_inc(eps_ready, 1)
                link.wait()
                own.mark(nc.vector.memset(zero_i, 0))
                own.mark(nc.vector.memset(ones, 1.0))
                dve.wait_ge(c_loaded, 64)
                link.mark(nc.vector.tensor_scalar(gain[:, 1:2], gain[:, 0:1], 1.0 - LAM_INIT, None, ALU.mult))
                dve.wait_ge(root_ready, 3)
                link.link(nc.vector.reciprocal(r_norm, r_norm))
                own.mark(nc.vector.scalar_tensor_tensor(out=diffT, in0=diffT, scalar=gain[:, 1:2], in1=r_norm,
                                                        op0=ALU.mult, op1=ALU.mult))
                for n, b in enumerate(order):
                    nt = BLOCKS[b][1]
                    r = res[0:nt, n % 2, :]
                    dve.wait_ge(x_again_loaded[b], 16)
                    dve.wait_ge(o_pe, 2 + n)
                    if b == 2:
                        dve.wait_ge(half_moved, 1)
                        link.mark(nc.vector.scalar_tensor_tensor(out=r[:, 0:512], in0=x_again[0:64, 2, 0:512],
                                                                 scalar=DEEP, in1=psum[0:64, 3, :],
                                                                 op0=ALU.mult, op1=ALU.add))
                        link.link(nc.vector.scalar_tensor_tensor(out=r[:, 512:1024], in0=x_again[0:64, 2, 512:1024],
                                                                 scalar=DEEP, in1=r[:, 512:1024],
                                                                 op0=ALU.mult, op1=ALU.add))
                    else:
                        k = 4 if b == 0 else 0
                        link.link(nc.vector.scalar_tensor_tensor(out=r, in0=x_again[:, b, :], scalar=DEEP,
                                                                 in1=psum[:, k:k + 2, :].rearrange("p n c -> p (n c)"),
                                                                 op0=ALU.mult, op1=ALU.add))
                    norm(dve, link, r, nt, n, x1[0:nt, b, :], 0, x1_ready, ln_loaded if n == 0 else None)
                link.mark(nc.vector.tensor_copy(token2_i, const["token2"]))
                for n, b in enumerate(order):
                    nt = BLOCKS[b][1]
                    dve.wait_ge(o_pe, 6 + 2 * n)
                    nc.vector.tensor_tensor(logits[0:nt, :], psum[0:nt, 2, 0:EXPERTS], b_route[0:nt, :], ALU.add
                                            ).then_inc(logits_read, 1)
                    dve.wait_ge(logits_read, n + 1)
                    link.link(nc.vector.max(top8[0:nt, b, :], logits[0:nt, :]))
                    nc.vector.tensor_scalar(norm_cols[0:nt, 24 + b:25 + b], top8[0:nt, b, 0:1], -1.0, None, ALU.mult
                                            ).then_inc(top_ready, 1)
                    link.link(nc.vector.max_index(idx8[0:nt, b, :], top8[0:nt, b, :], logits[0:nt, :]))
                    link.link(nc.vector.tensor_copy(which[0:nt, b, :], idx8[0:nt, b, 0:TOP_K]))
                    for k in range(TOP_K):
                        link.mark(nc.vector.tensor_scalar(hot[0:nt, b, k, :], const["expert"][0:nt, :],
                                                          which[0:nt, b, k:k + 1], None, ALU.is_equal))
                    link.wait()
                    nc.vector.tensor_reduce(picked[0:nt, b, :], hot[0:nt, b, :, :].rearrange("p k e -> p e k"),
                                            AX.X, ALU.add).then_inc(picked_ready, 1)
                for n, b in enumerate(order):
                    nt = BLOCKS[b][1]
                    dve.wait_ge(gate_ready, n + 1)
                    link.link(nc.vector.reciprocal(norm_cols[0:nt, 32 + b:33 + b], norm_cols[0:nt, 28 + b:29 + b]))
                    link.link(nc.vector.tensor_scalar(gates[0:nt, b, :], gates[0:nt, b, :],
                                                      norm_cols[0:nt, 32 + b:33 + b], None, ALU.mult))
                    for k in range(TOP_K):
                        if k == 0:
                            link.link(nc.vector.tensor_scalar(weight[0:nt, b, :], hot[0:nt, b, 0, :],
                                                              gates[0:nt, b, 0:1], None, ALU.mult))
                        else:
                            ins = nc.vector.scalar_tensor_tensor(out=weight[0:nt, b, :], in0=hot[0:nt, b, k, :],
                                                                 scalar=gates[0:nt, b, k:k + 1], in1=weight[0:nt, b, :],
                                                                 op0=ALU.mult, op1=ALU.add)
                            if k < TOP_K - 1:
                                link.link(ins)
                    ins.then_inc(weight_ready, 1)
                dve.wait_ge(o_pe, 11)
                link.link(nc.vector.tensor_copy(rank, psum[:, 3, 0:4 * EXPERTS].rearrange("p (b e) -> p b e", b=4)))
                sixties, item, at, first, tmp, tmp2 = work
                link.link(nc.vector.tensor_scalar(rank[:, 3, :], rank[:, 3, :], -1.0, None, ALU.add))
                link.link(nc.vector.tensor_scalar(sixties, rank, float(SLOTS), None, ALU.is_ge))
                for m in range(2, (TOKENS - 1) // SLOTS + 1):
                    link.link(nc.vector.scalar_tensor_tensor(out=sixties, in0=rank, scalar=float(m * SLOTS), in1=sixties,
                                                             op0=ALU.is_ge, op1=ALU.add))
                end, begin = first[:, 0, :], first[:, 1, :]
                link.link(nc.vector.tensor_tensor_scan(out=end, data0=one_col.to_broadcast([P, EXPERTS]),
                                                       data1=sixties[:, 3, :], initial=0.0, op0=ALU.mult, op1=ALU.add))
                link.link(nc.vector.tensor_tensor(begin, end, sixties[:, 3, :], ALU.subtract))
                link.mark(nc.vector.tensor_copy(count_i, end[:, EXPERTS - 1:EXPERTS]))
                link.link(nc.vector.scalar_tensor_tensor(out=tmp[:, 0, :], in0=begin, scalar=float(EXPERTS - 1),
                                                         in1=const["expert"], op0=ALU.add, op1=ALU.subtract))
                link.link(nc.vector.tensor_scalar(item, rank, float(SLOTS), None, ALU.is_ge))
                link.link(nc.vector.tensor_tensor(item, item, tmp[:, 0:1, :].to_broadcast([P, 4, EXPERTS]), ALU.mult))
                link.link(nc.vector.tensor_tensor(item, item, sixties, ALU.add))
                link.link(nc.vector.tensor_tensor(item, item, const["expert"].rearrange("p (o e) -> p o e", o=1)
                                                  .to_broadcast([P, 4, EXPERTS]), ALU.add))
                link.link(nc.vector.scalar_tensor_tensor(out=at, in0=sixties, scalar=-float(SLOTS), in1=rank,
                                                         op0=ALU.mult, op1=ALU.add))
                link.mark(nc.vector.scalar_tensor_tensor(out=tmp, in0=item, scalar=float(SLOTS), in1=at,
                                                         op0=ALU.mult, op1=ALU.add))
                link.link(nc.vector.scalar_tensor_tensor(out=tmp2, in0=at, scalar=float(TABLE_ITEMS), in1=item,
                                                         op0=ALU.mult, op1=ALU.add))
                for b in range(3):
                    nt = BLOCKS[b][1]
                    for i, t in ((1, tmp2), (0, tmp)):
                        link.link(nc.vector.tensor_tensor(hot_tmp[0:nt], hot[0:nt, b, :, :],
                                                          t[0:nt, b:b + 1, :].to_broadcast([nt, TOP_K, EXPERTS]),
                                                          ALU.mult))
                        link.link(nc.vector.tensor_reduce(places[0:nt, i, 4 * b:4 * b + 4], hot_tmp[0:nt], AX.X, ALU.add))
                    link.mark(nc.vector.tensor_copy(place_y[0:nt, 4 * b:4 * b + 4], places[0:nt, 0, 4 * b:4 * b + 4]))
                    nc.vector.tensor_copy(place_t[0:nt, 4 * b:4 * b + 4], places[0:nt, 1, 4 * b:4 * b + 4]
                                          ).then_inc(places_ready, 1)
                sel = item[:, 0, :]
                link.link(nc.vector.tensor_scalar(sel, begin, const["row"], None, ALU.is_le))
                link.link(nc.vector.tensor_scalar(at[:, 0, :], end, const["row"], None, ALU.is_gt))
                link.link(nc.vector.tensor_tensor(sel, sel, at[:, 0, :], ALU.mult))
                link.link(nc.vector.tensor_tensor(sel, sel, const["expert"], ALU.mult))
                link.link(nc.vector.tensor_reduce(extra_col[:, 0:1], sel, AX.X, ALU.add))
                nc.vector.tensor_copy(extra_i, extra_col[:, 0:1]).then_inc(extra_ready, 1)
                for i, b in enumerate((0, 1, 2)):
                    nt = BLOCKS[b][1]
                    dve.wait_ge(o_pe, 13 + i)
                    k = (4, 6, 4)[i]
                    nc.vector.scalar_tensor_tensor(out=base[0:nt, b, :], in0=x1[0:nt, b, :], scalar=DEEP,
                                                   in1=psum[0:nt, k:k + 2, :].rearrange("p n c -> p (n c)"),
                                                   op0=ALU.mult, op1=ALU.add).then_inc(base_ready, 1)
                dve.wait_ge(table_loaded, 32)
                nc.vector.tensor_scalar(idx_all, idx_all, const["half"], None, ALU.add).then_inc(idx_ready, 1)

            @block.gpsimd
            def _(pool):
                pool.wait_ge(o_dve, 1)
                table = slot_dram.rearrange("(s i) o -> s (i o)", s=SLOTS)
                pool.dma_start(table, zero_i[0:SLOTS, :]).then_inc(zeroed, 16)
                pool.wait_ge(zeroed, 16)
                for b in range(3):
                    nt = BLOCKS[b][1]
                    pool.wait_ge(places_ready, b + 1)
                    for k in range(TOP_K):
                        pool.indirect_dma_start(slot_dram, bass.IndirectOffsetOnAxis(
                            ap=place_t[0:nt, 4 * b + k:4 * b + k + 1], axis=0), token2_i[0:nt, b:b + 1], None
                            ).then_inc(placed, 16)
                pool.wait_ge(extra_ready, 1)
                pool.dma_start(extra_dram, extra_i[0:32, :]).then_inc(extra_stored, 16)
                pool.wait_ge(placed, 12 * 16)
                for h in range(2):
                    pool.dma_start(idx_all[64 * h:64 * h + 64, :], table).then_inc(table_loaded, 16)
                pool.wait_ge(extra_stored, 16)
                pool.wait_ge(x1_stored, 48)

        top[0] = kept_end
        xg = room(512)
        xgT = room(512)
        bias_row = room(2 * D)
        ones_row = room(SLOTS)
        gate_in, up_in, sig, hid, hidT, y_rows = (room(512) for _ in range(6))
        gathered, bias_loaded, xg_turned, xg_copied = (sem("gathered"), sem("bias_loaded"), sem("xg_turned"), sem("xg_copied"))
        bias_used, gate_up, hid_ready, hid_turned, hid_copied, down_done, y_copied, y_stored = (
            sem("bias_used"), sem("gate_up_done"), sem("hid_ready"), sem("hid_turned"), sem("hid_copied"),
            sem("down_done"), sem("y_copied"), sem("y_stored"))
        idx_seen = sem("idx_seen")
        w_used = [sem(f"w_used{s}") for s in range(RING)]
        gate_clamped, sig_ready, ones_ready, e_dve, idx_copied = (
            sem("gate_clamped"), sem("sig_ready"), sem("ones_ready"), sem("e_dve"), sem("idx_copied"))

        def items(eng, first, body):
            extras = eng.value_load(count_i[0:1, 0:1], min_val=0, max_val=MAX_EXTRA)
            with eng.Fori(first, EXPERTS) as t:
                body(t)
            with eng.Fori(0, MAX_EXTRA) as j:
                with eng.If(j < extras):
                    body(j + EXPERTS)

        with nc.Block() as block:
            @block.sync
            def _(sp):
                def load_bias(e):
                    sp.dma_start(bias_row[0:1, :], a["b_gate_up"][0, bass.ds(e, 1), :]).then_inc(bias_loaded, 16)

                def load_item(t, e):
                    for s in range(RING):
                        sp.wait_ge(w_used[s], t)
                        load_weights(sp, e, s)
                        if s == 0:
                            sp.wait_ge(bias_used, t)
                            load_bias(e)

                load_bias(0)
                extras = sp.value_load(count_i[0:1, 0:1], min_val=0, max_val=MAX_EXTRA)
                with sp.Fori(1, EXPERTS) as t:
                    load_item(t, t)
                with sp.Fori(0, MAX_EXTRA) as j:
                    with sp.If(j < extras):
                        load_item(j + EXPERTS, sp.value_load(extra_dram[bass.ds(j, 1), 0:1], min_val=0,
                                                             max_val=EXPERTS - 1))

            @block.gpsimd
            def _(pool):
                def gather(t):
                    nc.gpsimd.tensor_copy(idx_now, idx_all[:, bass.ds(t, 1)]).then_inc(idx_copied, 1)
                    pool.wait_ge(idx_copied, t + 1)
                    pool.sem_inc(idx_seen, 1)
                    pool.indirect_dma_start(xg, None, x1_dram,
                                            bass.IndirectOffsetOnAxis(ap=idx_now, axis=0)).then_inc(gathered, 16)

                gather(0)

                def body(t):
                    pool.wait_ge(xg_turned, t + 1)
                    gather(t + 1)
                items(pool, 0, body)

            @block.tensor
            def _(pe):
                def turn(t):
                    pe.wait_ge(gathered, 16 * t + 16)
                    for c in range(4):
                        ins = nc.tensor.transpose(psum[:, 2, c * P:(c + 1) * P], xg[:, c * P:(c + 1) * P], ident)
                    ins.then_inc(xg_turned, 1)

                turn(0)
                pe.wait_ge(ones_ready, 1)

                def body(t):
                    pe.wait_ge(xg_copied, t + 1)
                    pe.wait_ge(bias_loaded, 16 * t + 16)
                    for n in range(2):
                        for h in range(2):
                            col = n * D + h * 512
                            ins = nc.tensor.matmul(psum[64 * h:64 * h + 64, n, :], ones_row[0:1, :],
                                                   bias_row[0:1, col:col + 512], start=True, stop=False)
                    ins.then_inc(bias_used, 1)
                    for k in range(KD):
                        pe.wait_ge(w_loaded[k], 16 * t + 16)
                        x_k = xgT[:, (k % 4) * P + (k // 4) * 64:(k % 4) * P + (k // 4) * 64 + 64]
                        for n in range(2):
                            for h in range(2):
                                col = n * D + h * 512
                                ins = nc.tensor.matmul(psum[64 * h:64 * h + 64, n, :], x_k, slot[k][:, col:col + 512],
                                                       start=False, stop=(k == KD - 1))
                        ins.then_inc(w_used[k], 1)
                    turn(t + 1)
                    pe.wait_ge(hid_ready, t + 1)
                    for c in range(4):
                        ins = nc.tensor.transpose(psum[:, 3, c * P:(c + 1) * P], hid[:, c * P:(c + 1) * P], ident)
                    ins.then_inc(hid_turned, 1)
                    pe.wait_ge(hid_copied, t + 1)
                    for k in range(KD):
                        s, r = KD + k // 2, k % 2
                        if r == 0:
                            pe.wait_ge(w_loaded[s], 16 * t + 16)
                        h_k = hidT[:, (k % 4) * P + (k // 4) * 64:(k % 4) * P + (k // 4) * 64 + 64]
                        for h in range(2):
                            col = r * D + h * 512
                            ins = nc.tensor.matmul(psum[64 * h:64 * h + 64, 4, :], h_k, slot[s][:, col:col + 512],
                                                   start=(k == 0), stop=(k == KD - 1))
                        if r == 1:
                            ins.then_inc(w_used[s], 1)
                items(pe, 0, body)

            @block.scalar
            def _(act):
                act.sem_inc(y_stored, SEED)

                def body(t):
                    act.wait_ge(gate_clamped, t + 1)
                    nc.scalar.activation(sig, gate_in, ACT.Sigmoid, scale=SIG_ALPHA).then_inc(sig_ready, 1)
                    act.wait_ge(hid_turned, t + 1)
                    nc.scalar.activation(hidT, psum[:, 3, :], ACT.Copy).then_inc(hid_copied, 1)
                    act.wait_ge(w_used[RING - 1], t + 1)
                    act.wait_ge(y_stored, 32 * t + SEED)
                    nc.scalar.activation(y_rows, psum[:, 4, :], ACT.Copy).then_inc(y_copied, 1)
                    act.wait_ge(y_copied, t + 1)
                    for h in range(2):
                        act.dma_start(y_dram[bass.ds(t * SLOTS, SLOTS), h * 512:(h + 1) * 512],
                                      y_rows[64 * h:64 * h + 64, :]).then_inc(y_stored, 16)
                items(act, 0, body)

            @block.vector
            def _(dve):
                nc.vector.memset(ones_row[0:1, :], 1.0).then_inc(ones_ready, 1)

                def copy_x(t):
                    dve.wait_ge(xg_turned, t + 1)
                    nc.vector.tensor_copy(xgT, psum[:, 2, :]).then_inc(xg_copied, 1)

                copy_x(0)

                def body(t):
                    dve.wait_ge(w_used[KD - 1], t + 1)
                    nc.vector.tensor_scalar(gate_in, psum[:, 0, :], LIMIT, None, ALU.min).then_inc(gate_clamped, 1)
                    nc.vector.tensor_scalar(up_in, psum[:, 1, :], LIMIT, -LIMIT, ALU.min, ALU.max).then_inc(e_dve, 1)
                    dve.wait_ge(gate_clamped, t + 1)
                    dve.wait_ge(e_dve, 2 * t + 1)
                    nc.vector.scalar_tensor_tensor(out=up_in, in0=up_in, scalar=1.0, in1=gate_in,
                                                   op0=ALU.add, op1=ALU.mult).then_inc(e_dve, 1)
                    dve.wait_ge(e_dve, 2 * t + 2)
                    dve.wait_ge(sig_ready, t + 1)
                    nc.vector.tensor_tensor(hid, up_in, sig, ALU.mult).then_inc(hid_ready, 1)
                    copy_x(t + 1)
                items(dve, 0, body)

        picks = ring[:, 0:12 * D].rearrange("p (j d) -> p j d", j=12)
        picked_up = [sem(f"picked_up{b}") for b in range(3)]
        y_ready, y_out = sem("y_ready"), sem("y_out")
        top[0] = kept_end
        y_final = room(3 * D).rearrange("p (b d) -> p b d", b=3)
        f_std = sem("final_std")
        with nc.Block() as block:
            @block.gpsimd
            def _(pool):
                extras = pool.value_load(count_i[0:1, 0:1], min_val=0, max_val=MAX_EXTRA)
                pool.wait_ge(y_stored, 32 * extras + 32 * EXPERTS + SEED)
                pool.sem_inc(idx_seen, 1)
                for b in order:
                    nt = BLOCKS[b][1]
                    for k in range(TOP_K):
                        pool.indirect_dma_start(picks[0:nt, 4 * b + k, :], None, y_dram, bass.IndirectOffsetOnAxis(
                            ap=place_y[0:nt, 4 * b + k:4 * b + k + 1], axis=0)).then_inc(picked_up[b], 16)

            @block.scalar
            def _(act):
                for n, b in enumerate(order):
                    nt = BLOCKS[b][1]
                    act.wait_ge(var_ready, 3 + n + 1)
                    nc.scalar.activation(norm_cols[0:nt, 19 + n:20 + n], norm_cols[0:nt, 9 + 2 * n:10 + 2 * n], ACT.Sqrt,
                                         bias=norm_cols[0:nt, 0:1]).then_inc(std_ready, 1)

            @block.vector
            def _(dve):
                link = Count(dve, f_link)
                for n, b in enumerate(order):
                    nt = BLOCKS[b][1]
                    r = base[0:nt, b, :]
                    dve.wait_ge(picked_up[b], 64)
                    for k in range(TOP_K):
                        link.link(nc.vector.scalar_tensor_tensor(out=r, in0=picks[0:nt, 4 * b + k, :],
                                                                 scalar=gates[0:nt, b, k:k + 1], in1=r,
                                                                 op0=ALU.mult, op1=ALU.add))
                    norm(dve, link, r, nt, 3 + n, y_final[0:nt, b, :], 2, y_ready, None)

            @block.sync
            def _(sp):
                for n, b in enumerate(order):
                    sp.wait_ge(y_ready, n + 1)
                    sp.dma_start(out[("y", b)], y_final[0:BLOCKS[b][1], b, :]).then_inc(y_out, 16)
                sp.wait_ge(y_out, 48)


OUTS = [((1, PROMPT, D), "float32"), ((DEC_B, DEC_T, D), "float32"),
        ((1, 1, PROMPT, 8, HD), "float32"), ((1, 1, PROMPT, 8, HD), "float32"),
        ((1, 1, PROMPT, 4, 2, HD), "float32"), ((1, 1, PROMPT, 4, 2 * HD), "float32"),
        ((1, DEC_B, DEC_T, 8, HD), "float32"), ((1, DEC_B, DEC_T, 8, HD), "float32"),
        ((1, DEC_B, DEC_T, 4, 2, HD), "float32"), ((1, DEC_B, DEC_T, 4, 2 * HD), "float32")]


_INS = ["x_prompt", "x_sample", "cache_sb_k", "cache_sb_v", "cache_diff_k", "cache_diff_v", "page_table", "w_in",
        "lambda_q1", "lambda_k1", "lambda_q2", "lambda_k2", "subln_g", "w_out", "ln1_g", "ln1_b", "w_router",
        "b_router", "w_gate_up", "b_gate_up", "w_down", "b_down", "ln2_g", "ln2_b"]


def build(nc, inputs):
    arrays, a = {}, {}
    for name in _INS:
        v = np.ascontiguousarray(inputs[name])
        arrays[f"in_{name}"] = v
        a[name] = nc.dram_tensor(f"in_{name}", v.shape, mybir.dt.from_np(v.dtype), kind="ExternalInput").ap()
    arrays["constants"] = constants()
    consts = nc.dram_tensor("constants", (P, CONST_W), F32, kind="ExternalInput").ap()
    outs = [nc.dram_tensor(f"out_{i}", s, mybir.dt.from_np(np.dtype(t)), kind="ExternalOutput").ap()
            for i, (s, t) in enumerate(OUTS)]
    out = {("y", 2): outs[1].rearrange("b t d -> (b t) d")}
    for b in range(2):
        out[("y", b)] = outs[0][0, b * 128:b * 128 + 128, :]
    for i, what in enumerate(("sb_k", "sb_v", "diff_k", "diff_v")):
        flat = "a b t h c d -> (a b t) (h c d)" if what == "diff_k" else "a b t h d -> (a b t) (h d)"
        rows = outs[2 + i].rearrange(flat)
        for b in range(2):
            out[(what, b)] = rows[b * 128:b * 128 + 128, :]
        out[(what, 2)] = outs[6 + i].rearrange(flat)
    scratch = (nc.dram_tensor("x1_rows", (2 * TOKENS, D // 2), F32, kind="Internal").ap(),
               nc.dram_tensor("slot_tokens", (SLOTS * TABLE_ITEMS, 1), I32, kind="Internal").ap(),
               nc.dram_tensor("expert_rows", ((EXPERTS + MAX_EXTRA) * SLOTS, D), F32, kind="Internal").ap(),
               nc.dram_tensor("extra_items", (32, 1), I32, kind="Internal").ap())
    decoder_step(nc, a, out, consts, scratch)
    return arrays


def kernel(**inputs):
    import concourse.bacc as _bacc
    from concourse.bass_utils import run_bass_kernel_spmd as _run

    nc = _bacc.Bacc("TRN2", target_bir_lowering=False, num_devices=1)
    arrays = build(nc, inputs)
    r = _run(nc, [arrays], core_ids=[0])
    return tuple(r.results[0][f"out_{i}"] for i in range(len(OUTS)))
```

```python
from contextlib import ExitStack

import numpy as np
import concourse.bass as bass
from concourse import mybir

ALU = mybir.AluOpType
ACT = mybir.ActivationFunctionType
AX = mybir.AxisListType
F32 = mybir.dt.float32
I32 = mybir.dt.int32
U32 = mybir.dt.uint32

P = 128
D = 1024
KD = D // P
PROMPT, DEC_B, DEC_T = 256, 8, 8
SAMPLES = DEC_B * DEC_T
TOKENS = PROMPT + SAMPLES
BLOCKS = [(0, 128), (128, 128), (256, 64)]
PROJ = 3 * D
HD = 64
PAST, PAGE = 1024, 128
EXPERTS, TOP_K = 32, 4
SLOTS = 64
MAX_EXTRA = (TOKENS * TOP_K) // SLOTS - 1
GROUP = 4
TABLE_ITEMS = 64
BANK = 512
SLOT = 2048
RING = 12
SEED = 1
LIMIT, SIG_ALPHA = 7.0, 1.702
EPS = 1e-5
DEEP = 2.0 ** 0.25
LAM_INIT = 0.8 - 0.6
Q_SCALE = HD ** -0.5
NEG = -1e30
SLOPES = [2.0 ** (-8.0 * (h + 1) / 4) for h in range(4)]

CONST = {}
_at = 0
for _name, _n in (("ident", P), ("before", P), ("pdist", 256), ("pmask", 256), ("pneg", 256), ("sbias", PAST),
                  ("nbias", 120), ("nmask", 120), ("nneg", 120), ("slot", P), ("token2", 3),
                  ("half", 1), ("is_c0", 1), ("is_c1", 1), ("row", 1)):
    CONST[_name] = (_at, _n)
    _at += _n
CONST_W = _at


def constants():
    t = np.zeros((P, CONST_W), np.float32)

    def put(name, a):
        at, n = CONST[name]
        t[:, at:at + n] = a
    i, j = np.arange(P)[:, None], np.arange(P)[None, :]
    put("ident", i == j)
    put("before", i < j)
    k = np.arange(256)[None, :]
    put("pdist", np.where(k <= 128 + i, k - (128.0 + i), -1e35))
    put("pmask", k < 128 + i)
    put("pneg", np.where(k < 128 + i, 0.0, NEG))
    group, c, q = i // 32, (i % 32) // 8, i % 8
    real = c < 2
    slope = np.array(SLOPES)[group]
    put("sbias", np.where(real, slope * (np.arange(PAST)[None, :] - (PAST + q)), 0.0))
    n = np.arange(120)[None, :] - 56
    own = (n >= 0) & (n < 8)
    put("nbias", np.where(own & (n <= q), slope * (n - q), NEG))
    put("nmask", own & (n < q))
    put("nneg", np.where(own & (n < q), 0.0, NEG))
    put("slot", j % SLOTS)
    put("token2", 2 * (i + np.array([[b[0] for b in BLOCKS]])))
    put("half", i // 64)
    put("is_c0", c == 0)
    put("is_c1", c == 1)
    put("row", i)
    return t


class Count:

    def __init__(self, eng, sem):
        self.eng, self.sem, self.n, self.turn = eng, sem, 0, None

    def enter(self, turn, per, start=0):
        self.turn, self.per, self.first, self.start = turn, per, self.n, start

    def leave(self, turns):
        assert self.n - self.first == self.per, (self.sem, self.n - self.first, self.per)
        self.n = self.first + self.per * turns
        self.turn = None

    def wait(self, back=0):
        v = self.n - back
        self.eng.wait_ge(self.sem, v if self.turn is None else self.turn * self.per + (v - self.start * self.per))

    def next(self, k=1):
        self.n += k
        self.wait()

    def mark(self, ins, k=1):
        ins.then_inc(self.sem, k)
        self.n += k
        return self

    def link(self, ins):
        self.mark(ins)
        self.wait()


def decoder_step(nc, a, out, consts, scratch):
    x_dram = {0: a["x_prompt"][0, 0:128, :], 1: a["x_prompt"][0, 128:256, :],
              2: a["x_sample"].rearrange("b t d -> (b t) d")}
    w_in = a["w_in"][0]
    x1_dram, y_dram = scratch

    with ExitStack() as ctx:
        arena = ctx.enter_context(nc.sbuf_tensor("arena", [P, 52800], F32))
        small_i = ctx.enter_context(nc.sbuf_tensor("small_i", [P, 224], I32))
        psum = ctx.enter_context(nc.psum_tensor("psum", [P, 8, BANK], F32))
        top = [0]

        def sem(name):
            return ctx.enter_context(nc.semaphore(name))

        def room(n, at=None):
            start = top[0] if at is None else at
            if at is None:
                top[0] += n
            assert start + n <= 52800, start + n
            return arena[:, start:start + n]

        ring = room(RING * SLOT)
        slot = [ring[:, s * SLOT:(s + 1) * SLOT] for s in range(RING)]
        tab = room(CONST_W)
        mixT = room(8 * TOKENS).rearrange("p (k t) -> p k t", k=8)
        lam_cols = room(8)
        after_mix = top[0]
        const = {n: tab[:, at:at + w] for n, (at, w) in CONST.items()}
        ident = const["ident"]

        v_new = room(3 * D).rearrange("p (b d) -> p b d", b=3)
        qkT = room(4 * 4 * TOKENS).rearrange("p (n h t) -> p n h t", n=4, h=4)
        q_all = room(DEC_B * 2 * P).rearrange("p (b y r) -> p b y r", b=DEC_B, y=2)
        att_at = top[0]
        top[0] = att_at
        x_in = room(3 * D).rearrange("p (b d) -> p b d", b=3)
        xT = room(KD * TOKENS).rearrange("p (k t) -> p k t", k=KD)
        qk_rows = room(3 * 2 * D).rearrange("p (b d) -> p b d", b=3)
        proj_end = top[0]

        w_sem = [sem(f"w_in_loaded{k}") for k in range(KD)]
        x_loaded = [sem(f"x_loaded{b}") for b in range(3)]
        tab_loaded = sem("tab_loaded")
        ident_loaded = sem("ident_loaded")
        lam_loaded = sem("lam_loaded")
        pe_done = sem("pe_done")
        act_done = sem("act_done")
        dve_done = sem("dve_done")
        pool_done = sem("pool_done")
        w_in_used = sem("w_in_used")
        rows_out, last_rows_out = sem("rows_out"), sem("last_rows_out")
        page_loaded = [sem(f"page_loaded{s}") for s in range(8)]
        slot_used = {s: sem(f"slot_used{s}") for s in range(4, 8)}

        w_loaded = [sem(f"w_loaded{s}") for s in range(RING)]
        w_out_loaded = sem("w_out_loaded")
        turned = sem("turned")
        act_own, dve_own = sem("act_own"), sem("dve_own")
        caches = [a[n][0].rearrange(r) for n, r in (
            ("cache_sb_k", "n s h d -> n s (h d)"), ("cache_diff_k", "n s h c d -> n s (h c d)"),
            ("cache_sb_v", "n s h d -> n s (h d)"), ("cache_diff_v", "n s h d -> n s (h d)"))]
        TURNS = 22

        def past_used(sp, b, s):
            if s < 4:
                sp.wait_ge(turned, TURNS * b + ((4, 11, 18, 22)[s] - TURNS))
            else:
                sp.wait_ge(slot_used[s], b)

        def page_numbers(sp, b):
            return nc.values_load_multi_w_load_instructions(
                a["page_table"][bass.ds(b, 1), :], engines=[mybir.EngineType.SP], min_val=0,
                max_val=caches[0].shape[0] - 1)[1]

        def load_pages(sp, b, s, pages, reuse=False):
            if reuse:
                past_used(sp, b, s)
            for j, page in enumerate(pages[4 * (s % 2):4 * (s % 2) + 4]):
                sp.dma_start(slot[s][:, j * 512:(j + 1) * 512],
                             caches[s // 2][bass.ds(page, 1), :, :].rearrange("n s d -> (n s) d")
                             ).then_inc(page_loaded[s], 16)

        def load_weights(sp, e, s):
            if s < KD:
                src = a["w_gate_up"][0, bass.ds(e, 1), s * P:(s + 1) * P, :].rearrange("e p n -> (e p) n")
                dst = slot[s]
            else:
                j = s - KD
                src = a["w_down"][0, bass.ds(e, 1), 2 * j * P:(2 * j + 2) * P, :].rearrange("e (r p) n -> p (e r) n", p=P)
                dst = slot[s].rearrange("p (r n) -> p r n", r=2)
            sp.dma_start(dst, src).then_inc(w_loaded[s], 16)

        def rev(t, n):
            return t[:, 0:n][:, ::-1]

        def proj_dst(b, n, rows):
            if n in (2, 5):
                return v_new[rows, b, (n // 3) * 512:(n // 3) * 512 + 512]
            i = {0: 0, 1: 1, 3: 2, 4: 3}[n]
            return qk_rows[rows, b, i * 512:i * 512 + 512]

        NEW_ROWS = {1: "sb_k", 2: "sb_v", 4: "diff_k", 5: "diff_v"}
        lam_in = room(4 * HD, at=proj_end)
        lam_tmp = room(4 * HD, at=proj_end + 4 * HD)

        with nc.Block() as block:
            @block.sync
            def _(sp):
                sp.dma_start(ident, consts[:, 0:P]).then_inc(ident_loaded, 16)
                for b in (2, 0, 1):
                    sp.dma_start(x_in[0:BLOCKS[b][1], b, :], x_dram[b]).then_inc(x_loaded[b], 16)
                for k in range(KD):
                    sp.dma_start(ring[:, k * PROJ:(k + 1) * PROJ], w_in[k * P:(k + 1) * P, :]).then_inc(w_sem[k], 16)
                sp.dma_start(tab[:, P:], consts[:, P:]).then_inc(tab_loaded, 16)
                for i, n in enumerate(("lambda_q1", "lambda_k1", "lambda_q2", "lambda_k2")):
                    sp.dma_start(lam_in[:, i * HD:(i + 1) * HD], a[n].to_broadcast([P, HD])).then_inc(lam_loaded, 16)
                pages = page_numbers(sp, 0)
                for s in range(8):
                    sp.wait_ge(w_in_used, ((s + 1) * SLOT - 1) // PROJ + 1)
                    load_pages(sp, 0, s, pages)

            @block.tensor
            def _(pe):
                done = Count(pe, pe_done)
                evac = {"act": Count(pe, act_done), "dve": Count(pe, dve_done)}
                pe.wait_ge(ident_loaded, 16)
                for n, b in enumerate((2, 0, 1)):
                    t0, nt = BLOCKS[b]
                    pe.wait_ge(x_loaded[b], 16)
                    for g in range(2):
                        if n:
                            evac["act" if g == 0 else "dve"].next()
                        for c in range(4):
                            k = 4 * g + c
                            ins = nc.tensor.transpose(psum[:, 6 + g, c * P:c * P + nt],
                                                      x_in[0:nt, b, k * P:(k + 1) * P], ident[0:nt, 0:nt])
                        done.mark(ins)
                evac["act"].next()
                evac["dve"].next()
                bank_of = [3, 4, 5, 0, 1, 2]

                def prompt_columns(b, n, k):
                    col = k * PROJ + n * 512
                    return nc.tensor.matmul(psum[:, bank_of[n], :], xT[:, k, b * P:(b + 1) * P], ring[:, col:col + 512],
                                            start=(k == 0), stop=(k == KD - 1))

                for k in range(KD):
                    pe.wait_ge(w_sem[k], 16)
                    for n in range(3):
                        for h in range(2):
                            col = k * PROJ + (n + 3 * h) * 512
                            ins = nc.tensor.matmul(psum[64 * h:64 * h + 64, n, :], xT[:, k, 256:320],
                                                   ring[:, col:col + 512], start=(k == 0), stop=(k == KD - 1))
                    if k == KD - 1:
                        done.mark(ins)
                    for n in range(2):
                        ins = prompt_columns(0, n, k)
                        if k == KD - 1:
                            done.mark(ins)
                for n in range(2, 6):
                    if n == 3:
                        evac["act"].next(3)
                        evac["dve"].next(3)
                    for k in range(KD):
                        ins = prompt_columns(0, n, k)
                    done.mark(ins)

                def turn(n):
                    b, i = (2, 0, 1)[n // 4], n % 4
                    nt = BLOCKS[b][1]
                    for h in range(4):
                        ins = nc.tensor.transpose(psum[:, 6 + n % 2, h * P:h * P + nt],
                                                  qk_rows[0:nt, b, i * 512 + h * P:i * 512 + (h + 1) * P],
                                                  ident[0:nt, 0:nt])
                    done.mark(ins)

                turn(0)
                turn(1)
                evac["act"].next(3)
                evac["dve"].next(3)
                for n in range(2, 8):
                    evac["act" if n % 2 == 0 else "dve"].next()
                    turn(n)
                for k in range(KD):
                    for n in range(6):
                        ins = prompt_columns(1, n, k)
                    ins.then_inc(w_in_used, 1)
                evac["act"].next()
                evac["dve"].next()
                done.mark(nc.tensor.matmul(psum[:, 7, 0:1], xT[:, 0, 0:128], ident[:, 0:1], start=True, stop=True))
                evac["act"].next(3)
                evac["dve"].next(3)
                for n in range(8, 12):
                    if n >= 10:
                        evac["act" if n % 2 == 0 else "dve"].next()
                    turn(n)

            def projection_copies(eng, me, own):
                done = Count(eng, pe_done)

                def copy(dst, src, scale=1.0):
                    if me == 0:
                        return nc.scalar.activation(dst, src, ACT.Copy, scale=scale)
                    if scale == 1.0:
                        return nc.vector.tensor_copy(dst, src)
                    return nc.vector.tensor_scalar(dst, src, scale, None, ALU.mult)

                for b in (2, 0, 1):
                    t0, nt = BLOCKS[b]
                    done.next(2)
                    own.mark(copy(xT[:, 4 * me:4 * me + 4, t0:t0 + nt],
                                  psum[:, 6 + me, :].rearrange("p (c t) -> p c t", c=4)[:, :, 0:nt]))
                done.next()
                for n in range(3):
                    own.mark(copy(proj_dst(2, n + 3 * me, slice(0, 64)), psum[64 * me:64 * me + 64, n, :]))
                bank_of = [3, 4, 5, 0, 1, 2]
                for n in range(6):
                    done.next()
                    if n % 2 == me:
                        own.mark(copy(proj_dst(0, n, slice(0, 128)), psum[:, bank_of[n], :]))

                def copy_turned(n):
                    b, i = (2, 0, 1)[n // 4], n % 4
                    t0, nt = BLOCKS[b]
                    done.next()
                    if n % 2 != me:
                        return
                    src = psum[:, 6 + n % 2, :].rearrange("p (h t) -> p h t", h=4)[:, :, 0:nt]
                    scale = Q_SCALE if i % 2 == 0 else 1.0
                    if b == 2 and i % 2 == 0:
                        eng.wait_ge(pool_done, 1)
                        for c in range(2):
                            for h in range(4):
                                ins = copy(q_all[64 * c:64 * c + 64, :, i // 2, 32 * h + 8 * c:32 * h + 8 * c + 8],
                                           src[64 * c:64 * c + 64, h, :].rearrange("p (b q) -> p b q", b=DEC_B),
                                           scale)
                        own.mark(ins)
                    else:
                        own.mark(copy(qkT[:, i, :, t0:t0 + nt], src, scale))

                for n in range(8):
                    copy_turned(n)
                done.next()
                for n in range(6):
                    if n % 2 == me:
                        own.mark(copy(proj_dst(1, n, slice(0, 128)), psum[:, bank_of[n], :]))
                for n in range(8, 12):
                    copy_turned(n)

            @block.scalar
            def _(act):
                own = Count(act, act_done)
                projection_copies(act, 0, own)

            @block.vector
            def _(dve):
                own = Count(dve, dve_done)
                nc.vector.memset(v_new[64:128, 2, :], 0.0)
                projection_copies(dve, 1, own)
                dve.wait_ge(lam_loaded, 64)
                v = lam_in.rearrange("p (n j) -> p n j", n=4)
                own.link(nc.vector.tensor_tensor(lam_tmp[:, 0:2 * HD].rearrange("p (n j) -> p n j", n=2),
                                                 v[:, 0:4:2, :], v[:, 1:4:2, :], ALU.mult))
                own.mark(nc.vector.tensor_reduce(lam_cols[:, 0:2],
                                                 lam_tmp[:, 0:2 * HD].rearrange("p (n j) -> p n j", n=2),
                                                 AX.X, ALU.add))

            @block.gpsimd
            def _(pool):
                nc.gpsimd.memset(q_all, 0.0).then_inc(pool_done, 1)
                acts, dves = Count(pool, act_done), Count(pool, dve_done)
                acts.n, dves.n = 3, 3
                for b in (2, 0):
                    acts.next(3)
                    dves.next(3)
                    for n, what in NEW_ROWS.items():
                        pool.dma_start(out[(what, b)], proj_dst(b, n, slice(0, BLOCKS[b][1]))).then_inc(rows_out, 16)
        NK = PAST + SAMPLES
        NKP = PAST + P
        NCH = NKP // P
        top[0] = att_at
        kT = [room(4 * 512).rearrange("p (h k) -> p h k", h=4) for _ in range(2)]
        soft, stick, prob = room(NKP), room(NKP), room(NKP)
        wT = [room(NCH * P).rearrange("p (k r) -> p k r", k=NCH) for _ in range(2)]
        q_now = room(2 * P).rearrange("p (y r) -> p y r", y=2)
        o_rows = [room(P) for _ in range(2)]
        o_tmp = room(32).rearrange("p (h q) -> p h q", h=4)
        zeros = room(D)
        cols = room(64)
        one, neg_max, total, factor, coef, neg_lam, lam_e = (
            cols[:, 0:1], cols[:, 1:9], cols[:, 9:17], cols[:, 17:25], cols[:, 25:26], cols[:, 26:27], cols[:, 27:29])
        Z = [psum[:, 0:2, :].rearrange("p b c -> p (b c)"), psum[:, 2:4, :].rearrange("p b c -> p (b c)")]
        BY_KIND = (4, 7)
        ZN = [psum[:, n, 0:64] for n in BY_KIND]
        O = [psum[:, n, 128:256] for n in BY_KIND]
        OT = [psum[:, n, 256:384] for n in BY_KIND]
        copied = {"dve": sem("copied_dve"), "act": sem("copied_act")}
        scored = sem("scored")
        z_ready = [sem("z_sb_ready"), sem("z_diff_ready")]
        q_ready = sem("q_ready")
        log_ready = sem("log_ready")
        stick_ready = sem("stick_ready")
        w_ready = [sem("w_sb_ready"), sem("w_diff_ready")]
        max_ready = sem("max_ready")
        factor_ready = sem("factor_ready")
        mixed = [sem("mixed_sb"), sem("mixed_diff")]
        o_copied = [sem("o_sb_copied"), sem("o_diff_copied")]
        o_turned = [sem("o_sb_turned"), sem("o_diff_turned")]
        mix_stored = [sem("sb_stored"), sem("diff_stored")]
        setup_done, rows_zeroed = sem("setup_done"), sem("rows_zeroed")
        WHO = ["act" if j in (0, 1, 2, 3, 4, 7, 9, 11, 13, 17, 18, 19, 20, 21) else "dve" for j in range(TURNS)]
        PER_TURN = {e: WHO.count(e) for e in ("act", "dve")}

        def so_far(j, e=None):
            return WHO[:j + 1].count(e or WHO[j])

        KEYS, WEIGHTS = ((0, 1, 2, 3, 7, 8, 9, 10), tuple(range(14, 22))), ((4, 5, 6), (11, 12, 13))
        units = [(0, 0, 0, 8), (1, 0, 0, 8), (0, 1, 0, 4), (1, 1, 0, 4), (0, 1, 4, 4), (1, 1, 4, 4)]

        def place(nh, h):
            return (h % 2) * (nh // 2) + h // 2

        p_scored, p_turned, p_copied = sem("prompt_scored"), sem("prompt_turned"), sem("prompt_copied")
        p_log, p_stick, p_w = sem("prompt_log"), sem("prompt_stick"), [sem("prompt_sb_weights"), sem("prompt_diff_weights")]
        recip_done, first_half, reduced = sem("recip_done"), sem("first_half"), sem("reduced")
        p_exp, mix_part = sem("prompt_exp"), sem("mix_part")
        p_max, p_mixed, p_stored = sem("prompt_max"), sem("prompt_mixed"), sem("prompt_stored")
        p_free = sem("prompt_scores_used")

        with nc.Block() as block:
            def copy_bank(eng, turn, j):
                eng.wait_ge(turned, turn * TURNS + (j + 1))
                src = psum[:, 5 + j % 2, :]
                y = 0 if j in KEYS[0] + WEIGHTS[0] else 1
                if j in KEYS[y]:
                    n = KEYS[y].index(j)
                    eng.wait_ge(scored, 4 * turn + ((n // 4 + 1) * y + SEED))
                    dst, src = kT[n // 4][:, :, (n % 4) * P:(n % 4 + 1) * P], src.rearrange("p (h k) -> p h k", h=4)
                else:
                    n = WEIGHTS[y].index(j)
                    k0, k1 = 4 * n, min(4 * n + 4, NCH)
                    eng.wait_ge(mixed[y], turn - 1 + SEED)
                    dst, src = wT[y][:, k0:k1, :], src.rearrange("p (k r) -> p k r", k=4)[:, 0:k1 - k0, :]
                if WHO[j] == "dve":
                    nc.vector.tensor_copy(dst, src).then_inc(copied["dve"], 1)
                else:
                    nc.scalar.activation(dst, src, ACT.Copy).then_inc(copied["act"], 1)

            def banks(me, eng, turn, js):
                for j in js:
                    if WHO[j] == me:
                        copy_bank(eng, turn, j)

            def skip(me, eng, turn, js):
                k = sum(WHO[j] == me for j in js)
                if k:
                    before = turn * PER_TURN[me] + so_far(js[0], me) - (WHO[js[0]] == me)
                    eng.wait_ge(copied[me], before + SEED)
                    eng.sem_inc(copied[me], k)

            @block.sync
            def _(sp):
                for n, what in NEW_ROWS.items():
                    sp.dma_start(out[(what, 1)], proj_dst(1, n, slice(0, P))).then_inc(last_rows_out, 16)
                pages = page_numbers(sp, 1)
                for s in range(4):
                    load_pages(sp, 1, s, pages, True)
                with sp.Fori(2, DEC_B) as b:
                    pages, before = page_numbers(sp, b), page_numbers(sp, b - 1)
                    for s in (0, 4, 5, 1, 6, 7, 2, 3):
                        if s < 4:
                            load_pages(sp, b, s, pages, True)
                        else:
                            load_pages(sp, b - 1, s, before, True)
                before = page_numbers(sp, DEC_B - 1)
                for s in (0, 4, 5, 1, 6, 7, 2, 3):
                    if s < 4:
                        past_used(sp, DEC_B, s)
                        load_weights(sp, 0, s)
                    else:
                        load_pages(sp, DEC_B - 1, s, before, True)
                for j in range(4):
                    sp.dma_start(slot[8 + j].rearrange("p (r n) -> p r n", r=2),
                                 a["w_out"][0, 2 * j * P:(2 * j + 2) * P, :].rearrange("(r p) n -> p r n", p=P)
                                 ).then_inc(w_out_loaded, 16)
                for s in range(4, 8):
                    past_used(sp, DEC_B, s)
                    load_weights(sp, 0, s)

            @block.gpsimd
            def _(pool):
                pool.wait_ge(rows_out, 8 * 16)
                pool.wait_ge(last_rows_out, 4 * 16)
                nc.gpsimd.memset(prob[:, NK:], 0.0).then_inc(pool_done, 1)
                nc.gpsimd.memset(zeros, 0.0).then_inc(pool_done, 1)
                pool.wait_ge(pool_done, 3)
                pool.dma_start(y_dram[EXPERTS * SLOTS:, :].rearrange("(i s) d -> s i d", s=SLOTS),
                               zeros[0:SLOTS, :].rearrange("p (o d) -> p o d", o=1).to_broadcast([SLOTS, MAX_EXTRA, D])
                               ).then_inc(rows_zeroed, 16)
                with pool.Fori(0, DEC_B) as b:
                    pool.wait_ge(z_ready[1], b + SEED)
                    nc.gpsimd.tensor_copy(q_now, q_all[:, bass.ds(b, 1), :, :].rearrange("p b y r -> p (b y) r")
                                          ).then_inc(q_ready, 1)
                pool.wait_ge(rows_zeroed, 16)

            @block.tensor
            def _(pe):
                for s in (*z_ready, scored, *mixed, *o_turned):
                    pe.sem_inc(s, SEED)
                unused = {0: WEIGHTS[0] + WEIGHTS[1], DEC_B: KEYS[0] + KEYS[1]}

                def bank_free(turn, j):
                    last = j - 2
                    while isinstance(turn, int) and last in unused[turn]:
                        last -= 2
                    if last < 0 and isinstance(turn, int) and turn == 0:
                        return
                    e = WHO[last % TURNS]
                    n = so_far(last % TURNS) - (PER_TURN[e] if last < 0 else 0)
                    pe.wait_ge(copied[e], turn * PER_TURN[e] + (n + SEED))

                def bank_copied(turn, j):
                    pe.wait_ge(copied[WHO[j]], turn * PER_TURN[WHO[j]] + (so_far(j) + SEED))

                def turn_keys(b, y, pages):
                    for pg in pages:
                        j = KEYS[y][pg]
                        s = 2 * y + pg // 4
                        if pg % 4 == 0:
                            pe.wait_ge(page_loaded[s], 64 * b + 64)
                        bank_free(b, j)
                        for h in range(4):
                            at = (pg % 4) * 512 + h * P
                            ins = nc.tensor.transpose(psum[:, 5 + j % 2, h * P:(h + 1) * P],
                                                      slot[s][:, at:at + P], ident)
                        ins.then_inc(turned, 1)

                def score_keys(b, y):
                    if y == 0:
                        pe.wait_ge(q_ready, b + 1)
                        pe.wait_ge(stick_ready, 2 * b + SEED)
                    else:
                        pe.wait_ge(max_ready, b + SEED)
                    for c in range(2):
                        for e in ("act", "dve"):
                            js = [j for j in KEYS[y][4 * c:4 * c + 4] if WHO[j] == e]
                            if js:
                                bank_copied(b, js[-1])
                        for h in range(4):
                            ins = nc.tensor.matmul(Z[y][32 * h:32 * h + 32, c * 512:(c + 1) * 512],
                                                   q_now[:, y, 32 * h:32 * h + 32], kT[c][:, h, :],
                                                   start=True, stop=True)
                        ins.then_inc(scored, 1)
                    pe.wait_ge(mix_stored[y], b + SEED)
                    for h in range(4):
                        ins = nc.tensor.matmul(ZN[y][32 * h:32 * h + 32, :], q_now[:, y, 32 * h:32 * h + 32],
                                               qkT[:, 2 * y + 1, h, 256:320], start=True, stop=True)
                    ins.then_inc(z_ready[y], 1)

                def mix_values(b, y, turn):
                    pe.wait_ge(w_ready[y], b + 1)
                    for n, j in enumerate(WEIGHTS[y]):
                        bank_free(turn, j)
                        for k in range(4 * n, min(4 * n + 4, NCH)):
                            ins = nc.tensor.transpose(psum[:, 5 + j % 2, (k % 4) * P:(k % 4 + 1) * P],
                                                      (stick if y == 0 else prob)[:, k * P:(k + 1) * P], ident)
                        ins.then_inc(turned, 1)
                    for k in range(NCH):
                        if k % 4 == 0:
                            bank_copied(turn, WEIGHTS[y][k // 4])
                            if k < 8:
                                pe.wait_ge(page_loaded[4 + 2 * y + k // 4], 64 * b + 64)
                        for h in range(4):
                            if k < 8:
                                v = slot[4 + 2 * y + k // 4][:, (k % 4) * 512 + h * P:(k % 4) * 512 + (h + 1) * P]
                            else:
                                v = v_new[:, 2, y * 512 + h * P:y * 512 + (h + 1) * P]
                            ins = nc.tensor.matmul(O[y][32 * h:32 * h + 32, :], wT[y][:, k, 32 * h:32 * h + 32],
                                                   v, start=(k == 0), stop=(k == NCH - 1))
                        if k in (3, 7):
                            ins.then_inc(slot_used[4 + 2 * y + k // 4], 1)
                    ins.then_inc(mixed[y], 1)

                def turn_rows(b, y):
                    pe.wait_ge(o_copied[y], b + 1)
                    nc.tensor.transpose(OT[y], o_rows[y], ident).then_inc(o_turned[y], 1)

                turn_keys(0, 0, range(0, 4))
                pe.wait_ge(turned, 4)
                pe.sem_inc(turned, 3)
                turn_keys(0, 0, range(4, 8))
                score_keys(0, 0)
                pe.wait_ge(turned, 11)
                pe.sem_inc(turned, 3)
                turn_keys(0, 1, range(0, 8))
                score_keys(0, 1)
                with pe.Fori(1, DEC_B) as b:
                    turn_keys(b, 0, range(0, 4))
                    mix_values(b - 1, 0, b)
                    turn_keys(b, 0, range(4, 7))
                    turn_rows(b - 1, 0)
                    turn_keys(b, 0, range(7, 8))
                    score_keys(b, 0)
                    mix_values(b - 1, 1, b)
                    turn_keys(b, 1, range(0, 4))
                    turn_rows(b - 1, 1)
                    turn_keys(b, 1, range(4, 8))
                    score_keys(b, 1)
                pe.wait_ge(turned, DEC_B * TURNS)
                pe.sem_inc(turned, 4)
                mix_values(DEC_B - 1, 0, DEC_B)
                pe.wait_ge(turned, DEC_B * TURNS + 7)
                pe.sem_inc(turned, 4)
                turn_rows(DEC_B - 1, 0)
                mix_values(DEC_B - 1, 1, DEC_B)
                turn_rows(DEC_B - 1, 1)
                ztile = lambda u: Z[u % 2]

                def score(u):
                    y, qb, h0, nh = units[u]
                    width = 128 * (qb + 1)
                    if u >= 2:
                        pe.wait_ge(p_free, u - 1)
                    for h in range(nh):
                        hh, at = h0 + h, place(nh, h) * width
                        r = slice(64 * (hh % 2), 64 * (hh % 2) + 64)
                        ins = nc.tensor.matmul(ztile(u)[:, at:at + width],
                                               qkT[r, 2 * y, hh // 2, qb * P:(qb + 1) * P],
                                               qkT[r, 2 * y + 1, hh // 2, 0:width], start=True, stop=True)
                    ins.then_inc(p_scored, 1)

                turns = [0]

                def mix(u):
                    y, qb, h0, nh = units[u]
                    nkb = qb + 1
                    pe.wait_ge(p_w[y], u // 2 + 1)
                    for g in range(2 - y):
                        t = turns[0]
                        if t >= 2:
                            pe.wait_ge(p_copied, t - 1)
                        for c in range(4):
                            ins = nc.tensor.transpose(psum[:, 5 + t % 2, c * P:(c + 1) * P],
                                                      (stick if y == 0 else prob)[:, (4 * g + c) * P:(4 * g + c + 1) * P],
                                                      ident)
                        ins.then_inc(p_turned, 1)
                        turns[0] += 1
                    pe.wait_ge(p_copied, turns[0])
                    if y == 0 and u > 0 and h0 == 0:
                        pe.wait_ge(p_stored, 1)
                    if y == 1 and u > 1 and h0 == 0:
                        pe.wait_ge(p_stored, 2)
                    n_out = nh // (1 + y)
                    for h in range(n_out):
                        hh = h0 // (1 + y) + h
                        for kb in range(nkb):
                            if y == 0:
                                dst = psum[64 * (hh % 2):64 * (hh % 2) + 64, 4, (hh // 2) * P:(hh // 2 + 1) * P]
                                v = v_new[:, kb, hh * HD:(hh + 1) * HD]
                            else:
                                dst = psum[:, 7, hh * P:(hh + 1) * P]
                                v = v_new[:, kb, 512 + hh * P:512 + (hh + 1) * P]
                            ins = nc.tensor.matmul(dst, v, wT[y][:, (place(nh, h) if y == 0 else h) * nkb + kb, :],
                                                   start=(kb == 0), stop=(kb == nkb - 1))
                    ins.then_inc(p_mixed, 1)

                pe.wait_ge(stick_ready, 2 * DEC_B + SEED)
                score(0)
                pe.wait_ge(max_ready, DEC_B + SEED)
                for e in ("act", "dve"):
                    pe.wait_ge(copied[e], DEC_B * PER_TURN[e] + so_far(13, e) + SEED)
                pe.wait_ge(mix_stored[0], DEC_B + SEED)
                pe.wait_ge(mix_stored[1], DEC_B + SEED)
                score(1)
                for u in range(6):
                    if u + 2 < 6:
                        score(u + 2)
                    mix(u)

            @block.scalar
            def _(act):
                own = Count(act, act_own)
                act.sem_inc(copied["act"], SEED)
                nc.scalar.activation(lam_e, lam_cols[:, 0:2], ACT.Exp).then_inc(setup_done, 1)

                def rows(b, y):
                    act.wait_ge(mixed[y], b + 1 + SEED)
                    act.wait_ge(o_turned[y], b + SEED)
                    if y:
                        act.wait_ge(factor_ready, b + 1)
                    nc.scalar.activation(o_rows[y], O[y], ACT.Copy, scale=factor[:, 0:1] if y else 1.0
                                         ).then_inc(o_copied[y], 1)

                def weights(b, y):
                    if y == 0:
                        act.wait_ge(stick_ready, 2 * b + 2 + SEED)
                        nc.scalar.activation(stick[:, 0:NK], stick[:, 0:NK], ACT.Exp).then_inc(w_ready[0], 1)
                    else:
                        act.wait_ge(max_ready, b + 1 + SEED)
                        nc.scalar.activation(prob[:, 0:NK], prob[:, 0:NK], ACT.Exp, bias=neg_max[:, 0:1],
                                             accum_out=total[:, 0:1]).then_inc(w_ready[1], 1)

                def turn(b, first=False):
                    own.enter(b, 4, 0 if first else 1)
                    mine = lambda *js: banks("act", act, b, js)
                    mine(0, 1, 2)
                    if not first:
                        weights(b - 1, 0)
                    mine(3)
                    if first:
                        skip("act", act, b, (4, 5, 6))
                    else:
                        mine(4, 5, 6)
                    mine(7)
                    if not first:
                        weights(b - 1, 1)
                        rows(b - 1, 0)
                    mine(8, 9, 10)
                    if first:
                        skip("act", act, b, (11, 12, 13))
                    else:
                        mine(11, 12, 13)
                    act.wait_ge(z_ready[0], b + 1 + SEED)
                    if first:
                        act.wait_ge(rows_out, 8 * 16)
                        act.wait_ge(last_rows_out, 4 * 16)
                    own.mark(nc.scalar.activation(soft[:, 0:PAST], Z[0], ACT.Abs))
                    own.link(nc.scalar.activation(soft[:, PAST:NK], ZN[0], ACT.Abs))
                    own.link(nc.scalar.activation(soft[:, 0:NK], soft[:, 0:NK], ACT.Exp, scale=-1.0))
                    nc.scalar.activation(soft[:, 0:NK], soft[:, 0:NK], ACT.Ln, bias=1.0).then_inc(log_ready, 1)
                    mine(14, 15, 16)
                    if not first:
                        rows(b - 1, 1)
                    mine(17, 18, 19, 20, 21)
                    own.link(nc.scalar.activation(lam_e[:, 0:1], lam_cols[:, 0:1], ACT.Exp))

                turn(0, first=True)
                own.leave(1)
                with act.Fori(1, DEC_B) as b:
                    turn(b)
                    own.leave(DEC_B - 1)
                skip("act", act, DEC_B, (0, 1, 2, 3))
                weights(DEC_B - 1, 0)
                banks("act", act, DEC_B, (4, 5, 6))
                skip("act", act, DEC_B, (7, 8, 9, 10))
                weights(DEC_B - 1, 1)
                rows(DEC_B - 1, 0)
                banks("act", act, DEC_B, (11, 12, 13))
                rows(DEC_B - 1, 1)

                def softplus(u):
                    act.wait_ge(p_scored, u + 1)
                    if u:
                        act.wait_ge(p_stick, u // 2)
                    own.link(nc.scalar.activation(soft[:, 0:PAST], Z[u % 2], ACT.Abs))
                    own.link(nc.scalar.activation(soft[:, 0:PAST], soft[:, 0:PAST], ACT.Exp, scale=-1.0))
                    nc.scalar.activation(soft[:, 0:PAST], soft[:, 0:PAST], ACT.Ln, bias=1.0).then_inc(p_log, 1)

                def prompt_weights(u):
                    y, qb, h0, nh = units[u]
                    width = 128 * (qb + 1)
                    if y == 0:
                        act.wait_ge(p_stick, u // 2 + 1)
                        nc.scalar.activation(stick[:, 0:PAST], stick[:, 0:PAST], ACT.Exp).then_inc(p_w[y], 1)
                    else:
                        act.wait_ge(p_max, u // 2 + 1)
                        for h in range(nh):
                            nc.scalar.activation(prob[:, h * width:(h + 1) * width],
                                                 prob[:, h * width:(h + 1) * width], ACT.Exp,
                                                 bias=neg_max[:, h:h + 1], accum_out=total[:, h:h + 1]
                                                 ).then_inc(p_exp, 1)

                def copy_prompt(u):
                    y = units[u][0]
                    if u >= 2:
                        act.wait_ge(p_mixed, u - 1)
                    for g in range(2 - y):
                        t = 3 * (u // 2) + 2 * y + g
                        act.wait_ge(p_turned, t + 1)
                        nc.scalar.activation(wT[y][:, 4 * g:4 * g + 4, :],
                                             psum[:, 5 + t % 2, :].rearrange("p (k r) -> p k r", k=4), ACT.Copy
                                             ).then_inc(p_copied, 1)

                softplus(0)
                for u in (0, 2, 4):
                    prompt_weights(u)
                    prompt_weights(u + 1)
                    copy_prompt(u)
                    if u < 4:
                        softplus(u + 2)
                    copy_prompt(u + 1)

            @block.vector
            def _(dve):
                own = Count(dve, dve_own)
                for s in (copied["dve"], stick_ready, max_ready, *mix_stored):
                    dve.sem_inc(s, SEED)
                own.mark(nc.vector.memset(one, 1.0))
                dve.wait_ge(setup_done, 1)
                own.link(nc.vector.tensor_tensor(neg_lam, lam_e[:, 1:2], lam_e[:, 0:1], ALU.subtract))
                own.link(nc.vector.tensor_scalar(neg_lam, neg_lam, -LAM_INIT, None, ALU.add))
                own.link(nc.vector.scalar_tensor_tensor(out=coef, in0=const["is_c1"], scalar=neg_lam,
                                                        in1=const["is_c0"], op0=ALU.mult, op1=ALU.add))
                dve.wait_ge(tab_loaded, 16)
                dve.wait_ge(rows_out, 8 * 16)
                dve.wait_ge(last_rows_out, 4 * 16)
                own.mark(nc.vector.memset(stick[:, NK:], 0.0))

                def factors(b):
                    dve.wait_ge(w_ready[1], b + 1)
                    nc.vector.reciprocal(factor[:, 1:2], total[:, 0:1]).then_inc(recip_done, 1)
                    dve.wait_ge(recip_done, b + 1)
                    nc.vector.tensor_tensor(factor[:, 0:1], factor[:, 1:2], coef, ALU.mult).then_inc(factor_ready, 1)

                def store_rows(b, y):
                    tok = bass.ds(PROMPT + 8 * b, DEC_T)
                    dve.wait_ge(o_turned[y], b + 1 + SEED)
                    t = OT[y].rearrange("p (h r) -> p h r", h=4)
                    if y == 0:
                        nc.vector.tensor_copy(mixT[0:64, 0:4, tok], t[0:64, :, 0:8]).then_inc(first_half, 1)
                        nc.vector.tensor_copy(mixT[64:128, 0:4, tok], t[64:128, :, 8:16]).then_inc(mix_stored[0], 1)
                    else:
                        nc.vector.tensor_copy(o_tmp, t[:, :, 0:8]).then_inc(mix_part, 1)
                        dve.wait_ge(mix_part, b + 1)
                        nc.vector.tensor_tensor(mixT[:, 4:8, tok], t[:, :, 8:16], o_tmp, ALU.add
                                                ).then_inc(mix_stored[1], 1)

                def maxima(b, step):
                    if step == 0:
                        dve.wait_ge(z_ready[1], b + 1 + SEED)
                        nc.vector.tensor_tensor(prob[:, 0:PAST], Z[1], const["sbias"], ALU.add).then_inc(reduced, 1)
                        nc.vector.tensor_tensor(prob[:, PAST:NK], ZN[1], own_keys(b, "nbias"), ALU.add
                                                ).then_inc(reduced, 1)
                    else:
                        dve.wait_ge(reduced, 3 * b + 2)
                        nc.vector.tensor_reduce(neg_max[:, 1:2], prob[:, 0:NK], AX.X, ALU.max).then_inc(reduced, 1)
                        dve.wait_ge(reduced, 3 * b + 3)
                        nc.vector.tensor_scalar(neg_max[:, 0:1], neg_max[:, 1:2], -1.0, None, ALU.mult
                                                ).then_inc(max_ready, 1)

                own_keys = lambda b, n: const[n][:, bass.ds(56 - 8 * b, SAMPLES)]

                def turn(b, first=False):
                    own.enter(b, 5, 0 if first else 1)
                    mine = lambda *js: banks("dve", dve, b, js)
                    if not first:
                        maxima(b - 1, 0)
                        maxima(b - 1, 1)
                    mine(0, 1, 2, 3)
                    if first:
                        skip("dve", dve, b, (4, 5, 6))
                    else:
                        mine(4, 5, 6)
                    mine(7, 8)
                    if not first:
                        store_rows(b - 1, 0)
                    mine(9, 10)
                    if first:
                        skip("dve", dve, b, (11, 12, 13))
                    else:
                        mine(11, 12, 13)
                        factors(b - 1)
                    mine(14, 15, 16)
                    dve.wait_ge(log_ready, b + 1)
                    own.mark(nc.vector.scalar_tensor_tensor(out=soft[:, 0:PAST], in0=Z[0], scalar=0.0,
                                                            in1=soft[:, 0:PAST], op0=ALU.max, op1=ALU.add))
                    own.link(nc.vector.scalar_tensor_tensor(out=soft[:, PAST:NK], in0=ZN[0], scalar=0.0,
                                                            in1=soft[:, PAST:NK], op0=ALU.max, op1=ALU.add))
                    own.link(nc.vector.tensor_tensor(soft[:, PAST:NK], soft[:, PAST:NK], own_keys(b, "nmask"), ALU.mult))
                    own.link(nc.vector.tensor_tensor_scan(out=rev(stick, NK), data0=one.to_broadcast([P, NK]),
                                                          data1=rev(soft, NK), initial=0.0,
                                                          op0=ALU.mult, op1=ALU.add))
                    if not first:
                        store_rows(b - 1, 1)
                    nc.vector.tensor_tensor(stick[:, 0:PAST], Z[0], stick[:, 0:PAST], ALU.subtract
                                            ).then_inc(stick_ready, 1)
                    own.link(nc.vector.tensor_tensor(stick[:, PAST:NK], ZN[0], stick[:, PAST:NK], ALU.subtract))
                    nc.vector.tensor_tensor(stick[:, PAST:NK], stick[:, PAST:NK], own_keys(b, "nneg"), ALU.add
                                            ).then_inc(stick_ready, 1)

                turn(0, first=True)
                own.leave(1)
                with dve.Fori(1, DEC_B) as b:
                    turn(b)
                    own.leave(DEC_B - 1)
                maxima(DEC_B - 1, 0)
                maxima(DEC_B - 1, 1)
                skip("dve", dve, DEC_B, (0, 1, 2, 3))
                banks("dve", dve, DEC_B, (4, 5, 6))
                skip("dve", dve, DEC_B, (7, 8, 9, 10))
                store_rows(DEC_B - 1, 0)
                banks("dve", dve, DEC_B, (11, 12, 13))
                factors(DEC_B - 1)
                store_rows(DEC_B - 1, 1)
                exps = [0]

                def store(u):
                    y, qb, h0, nh = units[u]
                    dve.wait_ge(p_mixed, u + 1)
                    nc.vector.tensor_copy(mixT[:, 4 * y:4 * y + 4, qb * P:(qb + 1) * P],
                                          psum[:, 7 if y else 4, :].rearrange("p (h q) -> p h q", h=4)
                                          ).then_inc(p_stored, 1)

                for u, (y, qb, h0, nh) in enumerate(units):
                    width = 128 * (qb + 1)
                    heads = lambda t: t[:, 0:PAST].rearrange("p (h k) -> p h k", h=nh)
                    if y == 0:
                        own_block = lambda t: heads(t)[:, :, width - P:width]
                        over = lambda n: const[n][:, P:2 * P].rearrange("p (o k) -> p o k", o=1).to_broadcast([P, nh, P])
                        dve.wait_ge(p_log, u // 2 + 1)
                        own.link(nc.vector.scalar_tensor_tensor(out=soft[:, 0:PAST], in0=Z[u % 2], scalar=0.0,
                                                                in1=soft[:, 0:PAST], op0=ALU.max, op1=ALU.add))
                        own.link(nc.vector.tensor_tensor(own_block(soft), own_block(soft), over("pmask"), ALU.mult))
                        if u:
                            dve.wait_ge(p_turned, 3 * (u // 2 - 1) + 2)
                        for h in range(nh):
                            seg = slice(h * width, (h + 1) * width)
                            own.mark(nc.vector.tensor_tensor_scan(
                                out=rev(stick[:, seg], width), data0=one.to_broadcast([P, width]),
                                data1=rev(soft[:, seg], width), initial=0.0, op0=ALU.mult, op1=ALU.add))
                        own.wait()
                        nc.vector.tensor_tensor(stick[:, 0:PAST], Z[u % 2], stick[:, 0:PAST], ALU.subtract
                                                ).then_inc(p_free, 1)
                        dve.wait_ge(p_free, u + 1)
                        nc.vector.tensor_tensor(own_block(stick), own_block(stick), over("pneg"), ALU.add
                                                ).then_inc(p_stick, 1)
                        if u == 2:
                            store(0)
                    else:
                        tile = lambda n: const[n][:, 256 - width:256]
                        dve.wait_ge(p_scored, u + 1)
                        if u > 1:
                            dve.wait_ge(p_turned, 3 * (u // 2))
                        both = lambda t, h: t[:, 0:PAST].rearrange("p (c k) -> p c k", c=2)[:, :, h * width:(h + 1) * width]
                        for h in range(nh // 2):
                            ins = nc.vector.scalar_tensor_tensor(
                                out=both(prob, h),
                                in0=tile("pdist").rearrange("p (o k) -> p o k", o=1).to_broadcast([P, 2, width]),
                                scalar=SLOPES[h0 // 2 + h], in1=both(Z[u % 2], h), op0=ALU.mult, op1=ALU.add)
                            if h < nh // 2 - 1:
                                own.mark(ins)
                        ins.then_inc(p_free, 1)
                        own.wait()
                        dve.wait_ge(p_free, u + 1)
                        own.link(nc.vector.tensor_reduce(factor[:, 0:nh], heads(prob), AX.X, ALU.max))
                        nc.vector.tensor_scalar(neg_max[:, 0:nh], factor[:, 0:nh], -1.0, None, ALU.mult
                                                ).then_inc(p_max, 1)
                        if u == 3:
                            store(1)
                        exps[0] += nh
                        dve.wait_ge(p_exp, exps[0])
                        own.link(nc.vector.reciprocal(factor[:, 0:nh], total[:, 0:nh]))
                        own.link(nc.vector.tensor_scalar(factor[:, nh // 2:nh], factor[:, nh // 2:nh], neg_lam, None, ALU.mult))
                        for h in range(nh // 2):
                            s0 = slice(h * width, (h + 1) * width)
                            own.mark(nc.vector.tensor_scalar(prob[:, s0], prob[:, s0], factor[:, h:h + 1],
                                                             None, ALU.mult))
                        own.wait()
                        for h in range(nh // 2):
                            s0 = slice(h * width, (h + 1) * width)
                            s1 = slice(512 + h * width, 512 + (h + 1) * width)
                            own.mark(nc.vector.scalar_tensor_tensor(
                                out=prob[:, s0], in0=prob[:, s1], scalar=factor[:, nh // 2 + h:nh // 2 + h + 1],
                                in1=prob[:, s0], op0=ALU.mult, op1=ALU.add))
                        own.wait()
                        dve.sem_inc(p_w[y], 1)
                store(4)
                store(5)

        top[0] = after_mix
        x1 = room(3 * D).rearrange("p (b d) -> p b d", b=3)
        gates = room(12).rearrange("p (b k) -> p b k", b=3)
        norm_cols = room(64)
        hot = room(12 * EXPERTS).rearrange("p (b k e) -> p b k e", b=3, k=TOP_K)
        weight = room(3 * EXPERTS).rearrange("p (b e) -> p b e", b=3)
        ln_rows = room(4 * D).rearrange("p (n d) -> p n d", n=4)
        kept_end = top[0]
        x_again = room(3 * D).rearrange("p (b d) -> p b d", b=3)
        res = room(2 * D).rearrange("p (n d) -> p n d", n=2)
        x1T = room(KD * TOKENS).rearrange("p (k t) -> p k t", k=KD)
        w_route = room(KD * EXPERTS).rearrange("p (k e) -> p k e", k=KD)
        b_route = room(EXPERTS)
        gain = room(2)
        ones = room(P)
        top8 = room(3 * 8).rearrange("p (b k) -> p b k", b=3)
        which = room(3 * 4).rearrange("p (b k) -> p b k", b=3)
        logits = room(EXPERTS)
        picked = room(3 * EXPERTS).rearrange("p (b e) -> p b e", b=3)
        rank, sixties, item, at = (room(4 * EXPERTS).rearrange("p (n e) -> p n e", n=4) for _ in range(4))
        end, begin, first_item, started = (room(EXPERTS) for _ in range(4))
        hot_tmp = room(2 * TOP_K * EXPERTS).rearrange("p (j k e) -> p j k e", j=2, k=TOP_K)
        places = room(24).rearrange("p (j b k) -> p j b k", j=2, b=3)
        slot_hot = room(12 * P).rearrange("p (b k s) -> p b k s", b=3, k=TOP_K)
        item_hot = room(12 * TABLE_ITEMS).rearrange("p (b k i) -> p b k i", b=3, k=TOP_K)
        started_col = room(1)
        assert top[0] <= 52800
        squares, r_norm = x1T.rearrange("p k t -> p (k t)")[:, 0:4 * TOKENS], x1T.rearrange("p k t -> p (k t)")[:, 4 * TOKENS:]
        diffT = mixT[:, 4:8, :].rearrange("p h t -> p (h t)")

        idx_all = small_i[:, 0:64]
        place_y = small_i[:, 64:76].rearrange("p (b k) -> p b k", b=3)
        count_i, idx_now = small_i[:, 76:77], small_i[:, 77:78]
        first_i = small_i[:, 80:112]
        started_i = small_i[:, 112:176]
        idx8 = small_i[:, 176:200].bitcast(U32).rearrange("p (b k) -> p b k", b=3)

        c_loaded = sem("c_loaded")
        ln_loaded, x1_stored = sem("ln_loaded"), sem("x1_stored")
        order = (2, 0, 1)
        squared, ones_set, sums_done, root_ready, heads_normed = (
            sem("squared"), sem("ones_set"), sem("sums_done"), sem("root_ready"), sem("heads_normed"))
        projected = sem("projected")
        half_moved, var_ready, std_ready, eps_ready = (
            sem("half_moved"), sem("var_ready"), sem("std_ready"), sem("eps_ready"))
        x1_ready, x1_turned, x1_copied, logits_done = (
            sem("x1_ready"), sem("x1_turned"), sem("x1_copied"), sem("logits_done"))
        top_ready, gate_ready, logits_read, picked_ready = (
            sem("top_ready"), sem("gate_ready"), sem("logits_read"), sem("picked_ready"))
        ranked, places_hot, table_done, col_ready, col_turned, idx_ready = (
            sem("ranked"), sem("places_hot"), sem("table_done"), sem("col_ready"), sem("col_turned"), sem("idx_ready"))
        dve_link, f_link = sem("dve_link"), sem("final_link")
        one_col = ones[:, 0:1]
        links = []
        SUM_BANK = (6, 7, 2)
        PROJ_BANK = {0: 4, 1: 0}

        def norm(dve, link, r, nt, n, dst, g, ready, loaded, residual):
            m = n % 3
            stats = norm_cols[0:nt, 36:48].rearrange("p (c s) -> p c s", c=2)
            half = lambda c: slice(c * 512, (c + 1) * 512)
            for c in range(2):
                residual(c)
                link.mark(nc.vector.bn_stats(stats[:, c, :], r[:, half(c)]))
            link.wait()
            mean, var = norm_cols[0:nt, 8 + 2 * m:9 + 2 * m], norm_cols[0:nt, 9 + 2 * m:10 + 2 * m]
            nc.vector.bn_aggr(norm_cols[0:nt, 8 + 2 * m:10 + 2 * m], stats).then_inc(var_ready, 1)
            dve.wait_ge(std_ready, n + 1)
            root = norm_cols[0:nt, 16 + n:17 + n]
            link.link(nc.vector.reciprocal(root, root))
            for c in range(2):
                link.mark(nc.vector.tensor_scalar(r[:, half(c)], r[:, half(c)], mean, root, ALU.subtract, ALU.mult))
            if loaded is not None:
                dve.wait_ge(loaded, 64)
            for c in range(2):
                link.wait()
                link.link(nc.vector.tensor_tensor(r[:, half(c)], r[:, half(c)], ln_rows[0:nt, g, half(c)], ALU.mult))
                nc.vector.tensor_tensor(dst[:, half(c)], r[:, half(c)], ln_rows[0:nt, g + 1, half(c)], ALU.add
                                        ).then_inc(ready, 1)

        with nc.Block() as block:
            @block.sync
            def _(sp):
                for b in order:
                    sp.dma_start(x_again[0:BLOCKS[b][1], b, :], x_dram[b]).then_inc(x_loaded[b], 16)
                sp.dma_start(gain[:, 0:1], a["subln_g"].rearrange("o d -> d o")).then_inc(c_loaded, 16)
                sp.dma_start(w_route, a["w_router"][0].rearrange("(k p) e -> p k e", p=P)).then_inc(c_loaded, 16)
                sp.dma_start(b_route, a["b_router"].to_broadcast([P, EXPERTS])).then_inc(c_loaded, 16)
                for i, n in enumerate(("ln1_g", "ln1_b", "ln2_g", "ln2_b")):
                    sp.dma_start(ln_rows[:, i, :], a[n].to_broadcast([P, D])).then_inc(ln_loaded, 16)
                for s in range(8, RING):
                    sp.wait_ge(projected, 5)
                    load_weights(sp, 0, s)
                for n, b in enumerate(order):
                    sp.wait_ge(x1_ready, 2 * n + 2)
                    t0, nt = BLOCKS[b]
                    sp.dma_start(x1_dram[2 * t0:2 * (t0 + nt), :].rearrange("(t h) d -> t (h d)", h=2),
                                 x1[0:nt, b, :]).then_inc(x1_stored, 16)
                sp.wait_ge(x1_stored, 48)

            @block.tensor
            def _(pe):
                w_of = lambda k, n: slot[8 + k // 2][:, (k % 2) * D + n * 512:(k % 2) * D + n * 512 + 512]

                def project_samples(ks):
                    for k in ks:
                        for h in range(2):
                            ins = nc.tensor.matmul(psum[64 * h:64 * h + 64, 3, :], mixT[:, k, 256:320], w_of(k, h),
                                                   start=(k == 0), stop=(k == KD - 1))
                    return ins

                pe.wait_ge(w_out_loaded, 64)
                project_samples(range(0, 4))
                pe.wait_ge(squared, 1)
                pe.wait_ge(ones_set, 1)
                for n in range(3):
                    w = min(BANK, 4 * TOKENS - n * BANK)
                    ins = nc.tensor.matmul(psum[:, SUM_BANK[n], 0:w], ones, squares[:, n * BANK:n * BANK + w],
                                           start=True, stop=True)
                    ins.then_inc(sums_done, 1)
                def project(b, n, ks):
                    for k in ks:
                        ins = nc.tensor.matmul(psum[:, PROJ_BANK[b] + n, :], mixT[:, k, b * P:(b + 1) * P], w_of(k, n),
                                               start=(k == 0), stop=(k == KD - 1))
                    return ins

                def turn_x1(n):
                    b = order[n]
                    nt = BLOCKS[b][1]
                    for g in range(2):
                        pe.wait_ge(x1_ready, 2 * n + g + 1)
                        if n:
                            pe.wait_ge(x1_copied, 2 * n + g - 1)
                        for c in range(4):
                            k = 4 * g + c
                            ins = nc.tensor.transpose(psum[:, 6 + g, c * P:c * P + nt], x1[0:nt, b, k * P:(k + 1) * P],
                                                      ident[0:nt, 0:nt])
                        ins.then_inc(x1_turned, 1)

                def route(n):
                    t0, nt = BLOCKS[order[n]]
                    pe.wait_ge(x1_copied, 2 * n + 2)
                    if n:
                        pe.wait_ge(logits_read, n)
                    for k in range(KD):
                        ins = nc.tensor.matmul(psum[0:nt, 2, 0:EXPERTS], x1T[:, k, t0:t0 + nt], w_route[:, k, :],
                                               start=(k == 0), stop=(k == KD - 1))
                    ins.then_inc(logits_done, 1)

                project(0, 0, range(0, 4))
                project(0, 1, range(0, 4))
                pe.wait_ge(heads_normed, 1)
                project_samples(range(4, KD)).then_inc(projected, 1)
                project(0, 0, range(4, KD)).then_inc(projected, 1)
                project(0, 1, range(4, KD)).then_inc(projected, 1)
                turn_x1(0)
                project(1, 0, range(KD)).then_inc(projected, 1)
                pe.wait_ge(c_loaded, 48)
                route(0)
                turn_x1(1)
                project(1, 1, range(KD)).then_inc(projected, 1)
                route(1)
                turn_x1(2)
                route(2)
                for n in range(4):
                    for m in range(min(n + 1, 3)):
                        pe.wait_ge(picked_ready, m + 1)
                        nt = BLOCKS[order[m]][1]
                        ins = nc.tensor.matmul(psum[:, 3, n * EXPERTS:(n + 1) * EXPERTS],
                                               const["before"][0:nt, :] if m == n else ones[0:nt, :],
                                               picked[0:nt, order[m], :], start=(m == 0), stop=(m == min(n, 2)))
                ins.then_inc(ranked, 1)
                for n, b in enumerate(order):
                    nt = BLOCKS[b][1]
                    pe.wait_ge(places_hot, n + 1)
                    for k in range(TOP_K):
                        ins = nc.tensor.matmul(psum[:, 2, 0:TABLE_ITEMS], slot_hot[0:nt, b, k, :], item_hot[0:nt, b, k, :],
                                               start=(n == 0 and k == 0), stop=(n == 2 and k == TOP_K - 1))
                ins.then_inc(table_done, 1)
                pe.wait_ge(col_ready, 1)
                nc.tensor.matmul(psum[0:1, 4, 0:TABLE_ITEMS], started_col[0:TABLE_ITEMS, :],
                                 ident[0:TABLE_ITEMS, 0:TABLE_ITEMS], start=True, stop=True).then_inc(col_turned, 1)

            @block.scalar
            def _(act):
                act.wait_ge(eps_ready, 1)
                for n in range(3):
                    w = min(BANK, 4 * TOKENS - n * BANK)
                    act.wait_ge(sums_done, n + 1)
                    nc.scalar.activation(r_norm[:, n * BANK:n * BANK + w], psum[:, SUM_BANK[n], 0:w], ACT.Ln,
                                         scale=1.0 / P, bias=norm_cols[:, 0:1]).then_inc(root_ready, 1)
                act.wait_ge(root_ready, 3)
                nc.scalar.activation(r_norm, r_norm, ACT.Exp, scale=-0.5).then_inc(root_ready, 1)

                def std(n):
                    nt = BLOCKS[order[n]][1]
                    act.wait_ge(var_ready, n + 1)
                    nc.scalar.activation(norm_cols[0:nt, 16 + n:17 + n], norm_cols[0:nt, 9 + 2 * n:10 + 2 * n], ACT.Sqrt,
                                         bias=norm_cols[0:nt, 0:1]).then_inc(std_ready, 1)

                def copy_x1(n):
                    t0, nt = BLOCKS[order[n]]
                    for g in range(2):
                        act.wait_ge(x1_turned, 2 * n + g + 1)
                        nc.scalar.activation(x1T[:, 4 * g:4 * g + 4, t0:t0 + nt],
                                             psum[:, 6 + g, :].rearrange("p (c t) -> p c t", c=4)[:, :, 0:nt],
                                             ACT.Copy).then_inc(x1_copied, 1)

                act.wait_ge(projected, 1)
                nc.scalar.activation(res[0:64, 0, 512:1024], psum[64:128, 3, :], ACT.Copy).then_inc(half_moved, 1)
                std(0)
                std(1)
                copy_x1(0)
                copy_x1(1)
                std(2)
                copy_x1(2)
                for n, b in enumerate(order):
                    nt = BLOCKS[b][1]
                    act.wait_ge(top_ready, n + 1)
                    nc.scalar.activation(gates[0:nt, b, :], top8[0:nt, b, 0:TOP_K], ACT.Exp,
                                         bias=norm_cols[0:nt, 24 + b:25 + b],
                                         accum_out=norm_cols[0:nt, 28 + b:29 + b]).then_inc(gate_ready, 1)

            @block.vector
            def _(dve):
                link = Count(dve, dve_link)
                nc.vector.tensor_tensor(squares, diffT, diffT, ALU.mult).then_inc(squared, 1)
                nc.vector.memset(norm_cols[:, 0:1], EPS).then_inc(eps_ready, 1)
                nc.vector.memset(ones, 1.0).then_inc(ones_set, 1)
                dve.wait_ge(c_loaded, 48)
                link.link(nc.vector.tensor_scalar(gain[:, 1:2], gain[:, 0:1], 1.0 - LAM_INIT, None, ALU.mult))
                dve.wait_ge(root_ready, 4)
                nc.vector.scalar_tensor_tensor(out=diffT, in0=diffT, scalar=gain[:, 1:2], in1=r_norm,
                                               op0=ALU.mult, op1=ALU.mult).then_inc(heads_normed, 1)

                def norm_x1(n):
                    b = order[n]
                    nt = BLOCKS[b][1]
                    r = res[0:nt, n % 2, :]
                    dve.wait_ge(x_loaded[b], 32)

                    def residual(c):
                        cols_ = slice(c * 512, (c + 1) * 512)
                        if b == 2:
                            dve.wait_ge(projected, 1)
                            if c == 1:
                                dve.wait_ge(half_moved, 1)
                            mixer = psum[0:64, 3, :] if c == 0 else r[:, cols_]
                        else:
                            dve.wait_ge(projected, 2 * n + c)
                            mixer = psum[:, PROJ_BANK[b] + c, :]
                        link.link(nc.vector.scalar_tensor_tensor(out=r[:, cols_], in0=x_again[0:nt, b, cols_],
                                                                 scalar=DEEP, in1=mixer, op0=ALU.mult, op1=ALU.add))
                    norm(dve, link, r, nt, n, x1[0:nt, b, :], 0, x1_ready, ln_loaded if n == 0 else None, residual)

                def pick(n):
                    b = order[n]
                    nt = BLOCKS[b][1]
                    dve.wait_ge(logits_done, n + 1)
                    nc.vector.tensor_tensor(logits[0:nt, :], psum[0:nt, 2, 0:EXPERTS], b_route[0:nt, :], ALU.add
                                            ).then_inc(logits_read, 1)
                    dve.wait_ge(logits_read, n + 1)
                    link.link(nc.vector.max(top8[0:nt, b, :], logits[0:nt, :]))
                    link.link(nc.vector.max_index(idx8[0:nt, b, :], top8[0:nt, b, :], logits[0:nt, :]))
                    link.link(nc.vector.tensor_copy(which[0:nt, b, :], idx8[0:nt, b, 0:TOP_K]))
                    for k in range(TOP_K):
                        link.mark(nc.vector.tensor_scalar(hot[0:nt, b, k, :], const["slot"][0:nt, 0:EXPERTS],
                                                          which[0:nt, b, k:k + 1], None, ALU.is_equal))
                    link.wait()
                    nc.vector.tensor_reduce(picked[0:nt, b, :], hot[0:nt, b, :, :].rearrange("p k e -> p e k"),
                                            AX.X, ALU.add).then_inc(picked_ready, 1)
                    nc.vector.tensor_scalar(norm_cols[0:nt, 24 + b:25 + b], top8[0:nt, b, 0:1], -1.0, None, ALU.mult
                                            ).then_inc(top_ready, 1)

                norm_x1(0)
                norm_x1(1)
                pick(0)
                norm_x1(2)
                pick(1)
                pick(2)
                expert = const["slot"][:, 0:EXPERTS]
                each = lambda t: t.rearrange("p (o e) -> p o e", o=1).to_broadcast([P, 4, EXPERTS])
                dve.wait_ge(ranked, 1)
                link.mark(nc.vector.tensor_copy(rank[:, 0:3, :], psum[:, 3, 0:3 * EXPERTS].rearrange("p (n e) -> p n e", n=3)))
                link.link(nc.vector.tensor_scalar(rank[:, 3, :], psum[:, 3, 3 * EXPERTS:4 * EXPERTS], -1.0, None, ALU.add))
                link.link(nc.vector.tensor_scalar(sixties, rank, float(SLOTS), None, ALU.is_ge))
                for m in range(2, (TOKENS - 1) // SLOTS + 1):
                    link.link(nc.vector.scalar_tensor_tensor(out=sixties, in0=rank, scalar=float(m * SLOTS), in1=sixties,
                                                             op0=ALU.is_ge, op1=ALU.add))
                link.mark(nc.vector.scalar_tensor_tensor(out=at, in0=sixties, scalar=-float(SLOTS), in1=rank,
                                                         op0=ALU.mult, op1=ALU.add))
                link.link(nc.vector.tensor_tensor_scan(out=end, data0=one_col.to_broadcast([P, EXPERTS]),
                                                       data1=sixties[:, 3, :], initial=0.0, op0=ALU.mult, op1=ALU.add))
                link.link(nc.vector.tensor_tensor(begin, end, sixties[:, 3, :], ALU.subtract))
                link.link(nc.vector.tensor_tensor(first_item, begin, expert, ALU.add))
                link.link(nc.vector.tensor_tensor(item, sixties, each(first_item), ALU.add))
                for n, b in enumerate(order):
                    nt = BLOCKS[b][1]
                    for j, t in ((0, at), (1, item)):
                        link.mark(nc.vector.tensor_tensor(hot_tmp[0:nt, j], hot[0:nt, b, :, :],
                                                          t[0:nt, n:n + 1, :].to_broadcast([nt, TOP_K, EXPERTS]),
                                                          ALU.mult))
                    link.wait()
                    link.link(nc.vector.tensor_reduce(places[0:nt, :, b, :], hot_tmp[0:nt], AX.X, ALU.add))
                    for k in range(TOP_K):
                        link.mark(nc.vector.tensor_scalar(slot_hot[0:nt, b, k, :], const["slot"][0:nt, :],
                                                          places[0:nt, 0, b, k:k + 1], None, ALU.is_equal))
                        ins = nc.vector.tensor_scalar(item_hot[0:nt, b, k, :], const["slot"][0:nt, 0:TABLE_ITEMS],
                                                      places[0:nt, 1, b, k:k + 1], const["token2"][0:nt, b:b + 1],
                                                      ALU.is_equal, ALU.mult)
                        if k < TOP_K - 1:
                            link.mark(ins)
                    ins.then_inc(places_hot, 1)
                    link.wait()
                link.link(nc.vector.tensor_scalar(started, first_item, const["row"], None, ALU.is_le))
                nc.vector.tensor_reduce(started_col, started, AX.X, ALU.add).then_inc(col_ready, 1)
                link.mark(nc.vector.tensor_copy(count_i, end[:, EXPERTS - 1:EXPERTS]))
                link.mark(nc.vector.tensor_copy(first_i, first_item))
                dve.wait_ge(table_done, 1)
                nc.vector.tensor_scalar(idx_all, psum[:, 2, 0:TABLE_ITEMS], const["half"], None, ALU.add
                                        ).then_inc(idx_ready, 1)
                for rows_, b0, b1 in ((P, 0, 2), (SAMPLES, 2, 3)):
                    ins = nc.vector.scalar_tensor_tensor(
                        out=place_y[0:rows_, b0:b1, :], in0=places[0:rows_, 1, b0:b1, :], scalar=float(SLOTS),
                        in1=places[0:rows_, 0, b0:b1, :], op0=ALU.mult, op1=ALU.add)
                    link.mark(ins)
                dve.wait_ge(col_turned, 1)
                link.mark(nc.vector.tensor_scalar(started_i[0:1, :], psum[0:1, 4, 0:TABLE_ITEMS], 16.0, None, ALU.mult))
                links.append(link.n)

        top[0] = kept_end
        xg = room(512)
        xgT = room(512)
        bias_row = room(2 * D)
        ones_row = room(SLOTS)
        gate_in, up_in, sig, hid, hidT, y_rows = (room(512) for _ in range(6))
        b_down, weightT = room(D), room(3 * P).rearrange("p (b t) -> p b t", b=3)
        base = room(3 * D).rearrange("p (b d) -> p b d", b=3)
        gate_diag = room(8 * P).rearrange("p (b k t) -> p b k t", b=2, k=TOP_K)
        assert top[0] <= 52800
        b_down_loaded, weight_ready, weight_turned, weight_copied, bias_done, base_ready = (
            sem("b_down_loaded"), sem("weight_ready"), sem("weight_turned"), sem("weight_copied"), sem("bias_done"),
            sem("base_ready"))
        gathered, bias_loaded, xg_turned, xg_copied = (sem("gathered"), sem("bias_loaded"), sem("xg_turned"), sem("xg_copied"))
        bias_used, hid_ready, hid_turned, hid_copied, y_copied, y_stored = (
            sem("bias_used"), sem("hid_ready"), sem("hid_turned"), sem("hid_copied"), sem("y_copied"), sem("y_stored"))
        idx_seen = sem("idx_seen")
        w_used = [sem(f"w_used{s}") for s in range(RING)]
        gate_clamped, sig_ready, ones_ready, e_dve, idx_copied = (
            sem("gate_clamped"), sem("sig_ready"), sem("ones_ready"), sem("e_dve"), sem("idx_copied"))

        def warm(n):
            for _ in range(n):
                nc.tensor.matmul(psum[:, 7, :], ident, tab[:, 0:BANK], start=True, stop=True)

        def items(eng, body, midway=None):
            extras = eng.value_load(count_i[0:1, 0:1], min_val=0, max_val=MAX_EXTRA)
            if midway is None:
                with eng.Fori(0, EXPERTS) as t:
                    body(t)
            else:
                with eng.Fori(0, EXPERTS // 4) as t:
                    body(t)
                midway()
                with eng.Fori(EXPERTS // 4, EXPERTS) as t:
                    body(t)
            with eng.Fori(0, GROUP) as i:
                with eng.If(i < extras):
                    body(i + EXPERTS)
            with eng.If(extras > GROUP):
                with eng.Fori(GROUP, MAX_EXTRA) as i:
                    with eng.If(i < extras):
                        body(i + EXPERTS)
            return extras

        picks = ring[:, 0:12 * D].rearrange("p (j d) -> p j d", j=12)
        picked_up = [sem(f"picked_up{b}") for b in range(3)]
        y_ready, y_out = sem("y_ready"), sem("y_out")
        combined = sem("combined")
        COMBINED_BANK = (0, 3)

        with nc.Block() as block:
            @block.sync
            def _(sp):
                def load_bias(e):
                    sp.dma_start(bias_row[0:1, :], a["b_gate_up"][0, bass.ds(e, 1), :]).then_inc(bias_loaded, 16)

                load_bias(0)
                sp.dma_start(b_down[0:EXPERTS, :], a["b_down"][0]).then_inc(b_down_loaded, 16)
                with sp.Fori(1, EXPERTS) as e:
                    done = sp.value_load(first_i[0:1, bass.ds(e, 1)], min_val=1, max_val=EXPERTS + MAX_EXTRA)
                    for s in range(RING):
                        sp.wait_ge(w_used[s], done)
                        load_weights(sp, e, s)
                        if s == 0:
                            sp.wait_ge(bias_used, done)
                            load_bias(e)
                for n, b in enumerate(order):
                    for c in range(2):
                        cols_ = slice(c * 512, (c + 1) * 512)
                        sp.wait_ge(y_ready, 2 * n + c + 1)
                        sp.dma_start(out[("y", b)][:, cols_], base[0:BLOCKS[b][1], b, cols_]).then_inc(y_out, 16)
                sp.wait_ge(y_out, 6 * 16)

            @block.gpsimd
            def _(pool):
                def gather(t):
                    nc.gpsimd.tensor_copy(idx_now, idx_all[:, bass.ds(t, 1)]).then_inc(idx_copied, 1)
                    pool.wait_ge(idx_copied, t + 1)
                    pool.sem_inc(idx_seen, 1)
                    pool.indirect_dma_start(xg, None, x1_dram,
                                            bass.IndirectOffsetOnAxis(ap=idx_now, axis=0)).then_inc(gathered, 16)

                gather(0)

                def body(t):
                    pool.wait_ge(xg_turned, t + 1)
                    gather(t + 1)
                extras = items(pool, body)
                pool.wait_ge(y_stored, 32 * extras + 32 * EXPERTS + SEED)
                pool.sem_inc(idx_seen, 1)
                for b in order:
                    nt = BLOCKS[b][1]
                    for k in range(TOP_K):
                        pool.indirect_dma_start(picks[0:nt, 4 * b + k, :], None, y_dram, bass.IndirectOffsetOnAxis(
                            ap=place_y[0:nt, b, k:k + 1], axis=0)).then_inc(picked_up[b], 16)

            @block.tensor
            def _(pe):
                def turn(t):
                    pe.wait_ge(gathered, 16 * t + 16)
                    for c in range(4):
                        ins = nc.tensor.transpose(psum[:, 2, c * P:(c + 1) * P], xg[:, c * P:(c + 1) * P], ident)
                    ins.then_inc(xg_turned, 1)

                warm(2)
                turn(0)
                pe.wait_ge(ones_ready, 1)

                def body(t):
                    pe.wait_ge(xg_copied, t + 1)
                    loaded = pe.value_load(started_i[0:1, bass.ds(t, 1)], min_val=16, max_val=16 * EXPERTS)
                    pe.wait_ge(bias_loaded, loaded)
                    for n in range(2):
                        for h in range(2):
                            col = n * D + h * 512
                            ins = nc.tensor.matmul(psum[64 * h:64 * h + 64, n, :], ones_row[0:1, :],
                                                   bias_row[0:1, col:col + 512], start=True, stop=False)
                    ins.then_inc(bias_used, 1)
                    for k in range(KD):
                        pe.wait_ge(w_loaded[k], loaded)
                        x_k = xgT[:, (k % 4) * P + (k // 4) * 64:(k % 4) * P + (k // 4) * 64 + 64]
                        for n in range(2):
                            for h in range(2):
                                col = n * D + h * 512
                                ins = nc.tensor.matmul(psum[64 * h:64 * h + 64, n, :], x_k, slot[k][:, col:col + 512],
                                                       start=False, stop=(k == KD - 1))
                        ins.then_inc(w_used[k], 1)
                    turn(t + 1)
                    pe.wait_ge(hid_ready, t + 1)
                    for c in range(4):
                        ins = nc.tensor.transpose(psum[:, 3, c * P:(c + 1) * P], hid[:, c * P:(c + 1) * P], ident)
                    ins.then_inc(hid_turned, 1)
                    pe.wait_ge(hid_copied, t + 1)
                    for k in range(KD):
                        s, r = KD + k // 2, k % 2
                        if r == 0:
                            pe.wait_ge(w_loaded[s], loaded)
                        h_k = hidT[:, (k % 4) * P + (k // 4) * 64:(k % 4) * P + (k // 4) * 64 + 64]
                        for h in range(2):
                            col = r * D + h * 512
                            ins = nc.tensor.matmul(psum[64 * h:64 * h + 64, 4, :], h_k, slot[s][:, col:col + 512],
                                                   start=(k == 0), stop=(k == KD - 1))
                        if r == 1:
                            ins.then_inc(w_used[s], 1)

                def bias():
                    pe.wait_ge(weight_ready, 1)
                    for b in range(3):
                        nt = BLOCKS[b][1]
                        ins = nc.tensor.transpose(psum[0:EXPERTS, 7, b * P:b * P + nt], weight[0:nt, b, :],
                                                  ident[0:nt, 0:nt])
                    ins.then_inc(weight_turned, 1)
                    pe.wait_ge(b_down_loaded, 16)
                    pe.wait_ge(weight_copied, 3)
                    for n, b in enumerate(order):
                        nt = BLOCKS[b][1]
                        for c in range(2):
                            if n:
                                pe.wait_ge(base_ready, 2 * (n - 1) + c + 1)
                            nc.tensor.matmul(psum[0:nt, 5 + c, :], weightT[0:EXPERTS, b, 0:nt],
                                             b_down[0:EXPERTS, c * 512:(c + 1) * 512], start=True, stop=True
                                             ).then_inc(bias_done, 1)
                items(pe, body, bias)
                pe.wait_ge(base_ready, 6)
                pe.wait_ge(picked_up[order[0]], 64)
                warm(5)
                for b in range(2):
                    pe.wait_ge(picked_up[b], 64)
                    for c in range(2):
                        for k in range(TOP_K):
                            ins = nc.tensor.matmul(psum[:, COMBINED_BANK[b] + c, :], gate_diag[:, b, k, :],
                                                   picks[:, 4 * b + k, c * 512:(c + 1) * 512],
                                                   start=(k == 0), stop=(k == TOP_K - 1))
                        ins.then_inc(combined, 1)

            @block.scalar
            def _(act):
                act.sem_inc(y_stored, SEED)

                def body(t):
                    act.wait_ge(gate_clamped, t + 1)
                    nc.scalar.activation(sig, gate_in, ACT.Sigmoid, scale=SIG_ALPHA).then_inc(sig_ready, 1)
                    act.wait_ge(hid_turned, t + 1)
                    nc.scalar.activation(hidT, psum[:, 3, :], ACT.Copy).then_inc(hid_copied, 1)
                    act.wait_ge(w_used[RING - 1], t + 1)
                    act.wait_ge(y_stored, 32 * t + SEED)
                    nc.scalar.activation(y_rows, psum[:, 4, :], ACT.Copy).then_inc(y_copied, 1)
                    act.wait_ge(y_copied, t + 1)
                    for h in range(2):
                        act.dma_start(y_dram[bass.ds(t * SLOTS, SLOTS), h * 512:(h + 1) * 512],
                                      y_rows[64 * h:64 * h + 64, :]).then_inc(y_stored, 16)
                def copy_weights():
                    act.wait_ge(weight_turned, 1)
                    for b in range(3):
                        nt = BLOCKS[b][1]
                        nc.scalar.activation(weightT[0:EXPERTS, b, 0:nt], psum[0:EXPERTS, 7, b * P:b * P + nt], ACT.Copy
                                             ).then_inc(weight_copied, 1)
                items(act, body, copy_weights)
                for n, b in enumerate(order):
                    nt = BLOCKS[b][1]
                    act.wait_ge(var_ready, 3 + n + 1)
                    nc.scalar.activation(norm_cols[0:nt, 19 + n:20 + n], norm_cols[0:nt, 9 + 2 * n:10 + 2 * n], ACT.Sqrt,
                                         bias=norm_cols[0:nt, 0:1]).then_inc(std_ready, 1)

            @block.vector
            def _(dve):
                nc.vector.memset(ones_row[0:1, :], 1.0).then_inc(ones_ready, 1)

                def copy_x(t):
                    dve.wait_ge(xg_turned, t + 1)
                    nc.vector.tensor_copy(xgT, psum[:, 2, :]).then_inc(xg_copied, 1)

                copy_x(0)

                def body(t):
                    dve.wait_ge(w_used[KD - 1], t + 1)
                    nc.vector.tensor_scalar(gate_in, psum[:, 0, :], LIMIT, None, ALU.min).then_inc(gate_clamped, 1)
                    nc.vector.tensor_scalar(up_in, psum[:, 1, :], LIMIT, -LIMIT, ALU.min, ALU.max).then_inc(e_dve, 1)
                    dve.wait_ge(gate_clamped, t + 1)
                    dve.wait_ge(e_dve, 2 * t + 1)
                    nc.vector.scalar_tensor_tensor(out=up_in, in0=up_in, scalar=1.0, in1=gate_in,
                                                   op0=ALU.add, op1=ALU.mult).then_inc(e_dve, 1)
                    dve.wait_ge(e_dve, 2 * t + 2)
                    dve.wait_ge(sig_ready, t + 1)
                    nc.vector.tensor_tensor(hid, up_in, sig, ALU.mult).then_inc(hid_ready, 1)
                    copy_x(t + 1)

                def residuals():
                    link = Count(dve, dve_link)
                    link.n = links[0]
                    for b in order:
                        nt = BLOCKS[b][1]
                        link.link(nc.vector.reciprocal(norm_cols[0:nt, 32 + b:33 + b], norm_cols[0:nt, 28 + b:29 + b]))
                        link.link(nc.vector.tensor_scalar(gates[0:nt, b, :], gates[0:nt, b, :],
                                                          norm_cols[0:nt, 32 + b:33 + b], None, ALU.mult))
                        for k in range(TOP_K):
                            if k == 0:
                                ins = nc.vector.tensor_scalar(weight[0:nt, b, :], hot[0:nt, b, 0, :], gates[0:nt, b, 0:1],
                                                              None, ALU.mult)
                            else:
                                ins = nc.vector.scalar_tensor_tensor(out=weight[0:nt, b, :], in0=hot[0:nt, b, k, :],
                                                                     scalar=gates[0:nt, b, k:k + 1], in1=weight[0:nt, b, :],
                                                                     op0=ALU.mult, op1=ALU.add)
                            link.link(ins)
                            if b < 2:
                                link.mark(nc.vector.tensor_scalar(gate_diag[:, b, k, :], ident, gates[:, b, k:k + 1], None,
                                                                  ALU.mult))
                    link.wait()
                    dve.sem_inc(weight_ready, 1)
                    for n, b in enumerate(order):
                        nt = BLOCKS[b][1]
                        for c in range(2):
                            cols_ = slice(c * 512, (c + 1) * 512)
                            dve.wait_ge(bias_done, 2 * n + c + 1)
                            nc.vector.scalar_tensor_tensor(out=base[0:nt, b, cols_], in0=x1[0:nt, b, cols_], scalar=DEEP,
                                                           in1=psum[0:nt, 5 + c, :], op0=ALU.mult, op1=ALU.add
                                                           ).then_inc(base_ready, 1)
                items(dve, body, residuals)
                link = Count(dve, f_link)
                for n, b in enumerate(order):
                    nt = BLOCKS[b][1]
                    r = base[0:nt, b, :]

                    def residual(c):
                        cols_ = slice(c * 512, (c + 1) * 512)
                        if b < 2:
                            dve.wait_ge(combined, 2 * b + c + 1)
                            link.link(nc.vector.tensor_tensor(r[:, cols_], r[:, cols_], psum[:, COMBINED_BANK[b] + c, :], ALU.add))
                        else:
                            dve.wait_ge(picked_up[b], 64)
                            for k in range(TOP_K):
                                link.link(nc.vector.scalar_tensor_tensor(
                                    out=r[:, cols_], in0=picks[0:nt, 4 * b + k, cols_], scalar=gates[0:nt, b, k:k + 1],
                                    in1=r[:, cols_], op0=ALU.mult, op1=ALU.add))
                    norm(dve, link, r, nt, 3 + n, r, 2, y_ready, None, residual)


OUTS = [((1, PROMPT, D), "float32"), ((DEC_B, DEC_T, D), "float32"),
        ((1, 1, PROMPT, 8, HD), "float32"), ((1, 1, PROMPT, 8, HD), "float32"),
        ((1, 1, PROMPT, 4, 2, HD), "float32"), ((1, 1, PROMPT, 4, 2 * HD), "float32"),
        ((1, DEC_B, DEC_T, 8, HD), "float32"), ((1, DEC_B, DEC_T, 8, HD), "float32"),
        ((1, DEC_B, DEC_T, 4, 2, HD), "float32"), ((1, DEC_B, DEC_T, 4, 2 * HD), "float32")]


_INS = ["x_prompt", "x_sample", "cache_sb_k", "cache_sb_v", "cache_diff_k", "cache_diff_v", "page_table", "w_in",
        "lambda_q1", "lambda_k1", "lambda_q2", "lambda_k2", "subln_g", "w_out", "ln1_g", "ln1_b", "w_router",
        "b_router", "w_gate_up", "b_gate_up", "w_down", "b_down", "ln2_g", "ln2_b"]


def build(nc, inputs):
    arrays, a = {}, {}
    for name in _INS:
        v = np.ascontiguousarray(inputs[name])
        arrays[f"in_{name}"] = v
        a[name] = nc.dram_tensor(f"in_{name}", v.shape, mybir.dt.from_np(v.dtype), kind="ExternalInput").ap()
    arrays["constants"] = constants()
    consts = nc.dram_tensor("constants", (P, CONST_W), F32, kind="ExternalInput").ap()
    outs = [nc.dram_tensor(f"out_{i}", s, mybir.dt.from_np(np.dtype(t)), kind="ExternalOutput").ap()
            for i, (s, t) in enumerate(OUTS)]
    out = {("y", 2): outs[1].rearrange("b t d -> (b t) d")}
    for b in range(2):
        out[("y", b)] = outs[0][0, b * 128:b * 128 + 128, :]
    for i, what in enumerate(("sb_k", "sb_v", "diff_k", "diff_v")):
        flat = "a b t h c d -> (a b t) (h c d)" if what == "diff_k" else "a b t h d -> (a b t) (h d)"
        rows = outs[2 + i].rearrange(flat)
        for b in range(2):
            out[(what, b)] = rows[b * 128:b * 128 + 128, :]
        out[(what, 2)] = outs[6 + i].rearrange(flat)
    scratch = (nc.dram_tensor("x1_rows", (2 * TOKENS, D // 2), F32, kind="Internal").ap(),
               nc.dram_tensor("expert_rows", ((EXPERTS + MAX_EXTRA) * SLOTS, D), F32, kind="Internal").ap())
    decoder_step(nc, a, out, consts, scratch)
    return arrays


def kernel(**inputs):
    import concourse.bacc as _bacc
    from concourse.bass_utils import run_bass_kernel_spmd as _run

    nc = _bacc.Bacc("TRN2", target_bir_lowering=False, num_devices=1)
    arrays = build(nc, inputs)
    r = _run(nc, [arrays], core_ids=[0])
    return tuple(r.results[0][f"out_{i}"] for i in range(len(OUTS)))
```
